# Optimizing a Trainium2 kernel written in Bass

```python
import math
import jax
import jax.numpy as jnp
from jax import lax
import numpy as np

D_MODEL = 1024
BATCH = 1
SEQ = 512
DEPTH = 2

CHUNK = 64
EPS = 1e-6
N_BRANCH = 3
BRANCH_WIDTH = 512

DN_HEADS = 4
DN_DK = 128
DN_DV = 128
DN_CONV = 4
DN_QK = DN_HEADS * DN_DK
DN_VW = DN_HEADS * DN_DV
DN_QKV = 2 * DN_QK + DN_VW

RET_HEADS = 4
RET_DK = 64
RET_DV = 128
RET_QK = RET_HEADS * RET_DK
RET_VW = RET_HEADS * RET_DV
ROPE_BASE = 10000.0

LRU_WIDTH = 512
LRU_BLOCKS = 4
LRU_BLOCK = LRU_WIDTH // LRU_BLOCKS
LRU_CONV = 4
LRU_C = 8.0

D_FF = 2816
FFN_CONV = 3

IN_SIZES = (DN_QKV, DN_HEADS, DN_HEADS, DN_VW, RET_QK, RET_QK, RET_VW, RET_VW, LRU_WIDTH, LRU_WIDTH, N_BRANCH * D_MODEL)
N_IN = sum(IN_SIZES)

kernel_name = 'hybrid_deltanet_retention_rglru_convffn'

def _rms_norm(x, g):
    xf = x.astype(jnp.float32)
    y = xf * lax.rsqrt(jnp.mean(xf * xf, axis=-1, keepdims=True) + EPS)
    return (y * g.astype(jnp.float32)).astype(x.dtype)

def _l2norm(t):
    return t * lax.rsqrt(jnp.sum(t * t, axis=-1, keepdims=True) + EPS)

def _head_rms(t):
    return t * lax.rsqrt(jnp.mean(t * t, axis=-1, keepdims=True) + EPS)

def _head_groupnorm(t):
    mu = jnp.mean(t, axis=-1, keepdims=True)
    var = jnp.mean(jnp.square(t - mu), axis=-1, keepdims=True)
    return (t - mu) * lax.rsqrt(var + EPS)

def _causal_dwconv(x, w, b=None):
    width = w.shape[0]
    seq = x.shape[1]
    xp = jnp.pad(x, ((0, 0), (width - 1, 0), (0, 0)))
    y = xp[:, 0:seq, :] * w[0]
    for j in range(1, width):
        y = y + xp[:, j:j + seq, :] * w[j]
    return y if b is None else y + b

def _to_chunks(t, n):
    b, _, h, d = t.shape
    return t.reshape(b, n, CHUNK, h, d).transpose(0, 3, 1, 2, 4)

def _from_chunks(t):
    b, h, n, c, d = t.shape
    return t.transpose(0, 2, 3, 1, 4).reshape(b, n * c, h, d)

def _rotary(t, positions):
    half = t.shape[-1] // 2
    inv = ROPE_BASE ** (-jnp.arange(half, dtype=jnp.float32) / half)
    ang = positions.astype(jnp.float32)[:, :, None, None] * inv
    cos, sin = jnp.cos(ang), jnp.sin(ang)
    t1, t2 = t[..., :half], t[..., half:]
    return jnp.concatenate([t1 * cos - t2 * sin, t1 * sin + t2 * cos], axis=-1)

def _gated_delta_rule(q, k, v, g, beta):
    bsz, seq, nh, dk = q.shape
    dv = v.shape[-1]
    n = seq // CHUNK
    q = _l2norm(q) * (dk ** -0.5)
    k = _l2norm(k)
    q, k, v = _to_chunks(q, n), _to_chunks(k, n), _to_chunks(v, n)
    g = _to_chunks(g[..., None], n)[..., 0]
    beta = _to_chunks(beta[..., None], n)[..., 0]
    g = jnp.cumsum(g, axis=-1)
    causal = jnp.tril(jnp.ones((CHUNK, CHUNK), dtype=bool))
    strict = jnp.tril(jnp.ones((CHUNK, CHUNK), dtype=bool), -1)
    diff = g[..., :, None] - g[..., None, :]
    decay = jnp.where(causal, jnp.exp(jnp.where(causal, diff, 0.0)), 0.0)
    k_beta = k * beta[..., None]
    kk = jnp.einsum('bhnck,bhnsk->bhncs', k_beta, k)
    eye = jnp.eye(CHUNK, dtype=jnp.float32)
    lower = eye + jnp.where(strict, kk * decay, 0.0)
    t_inv = lax.linalg.triangular_solve(lower, jnp.broadcast_to(eye, lower.shape), left_side=True, lower=True)
    u = jnp.einsum('bhncs,bhnsv->bhncv', t_inv, v * beta[..., None])
    w = jnp.einsum('bhncs,bhnsk->bhnck', t_inv, k_beta * jnp.exp(g)[..., None])
    attn = jnp.einsum('bhnck,bhnsk->bhncs', q, k) * decay
    q_dec = q * jnp.exp(g)[..., None]
    k_dec = k * jnp.exp(g[..., -1:] - g)[..., None]
    g_end = jnp.exp(g[..., -1])

    def step(state, inp):
        qd, kd, uc, wc, ac, ge = inp
        v_new = uc - jnp.einsum('bhck,bhkv->bhcv', wc, state)
        out = jnp.einsum('bhck,bhkv->bhcv', qd, state) + jnp.einsum('bhcs,bhsv->bhcv', ac, v_new)
        state = state * ge[..., None, None] + jnp.einsum('bhck,bhcv->bhkv', kd, v_new)
        return state, out

    xs = (jnp.moveaxis(q_dec, 2, 0), jnp.moveaxis(k_dec, 2, 0), jnp.moveaxis(u, 2, 0),
          jnp.moveaxis(w, 2, 0), jnp.moveaxis(attn, 2, 0), jnp.moveaxis(g_end, 2, 0))
    s0 = jnp.zeros((bsz, nh, dk, dv), jnp.float32)
    _, out = lax.scan(step, s0, xs)
    return _from_chunks(jnp.moveaxis(out, 0, 2))

def _retention(q, k, v, log_gamma):
    bsz, seq, nh, dk = q.shape
    dv = v.shape[-1]
    n = seq // CHUNK
    k = k * (dk ** -0.5)
    q, k, v = _to_chunks(q, n), _to_chunks(k, n), _to_chunks(v, n)
    idx = jnp.arange(CHUNK, dtype=jnp.float32)
    dist = idx[:, None] - idx[None, :]
    causal = dist >= 0
    dmask = jnp.where(causal, jnp.exp(jnp.where(causal, dist, 0.0) * log_gamma[:, None, None]), 0.0)
    scores = jnp.einsum('bhnck,bhnsk->bhncs', q, k) * dmask[:, None]
    inner = jnp.einsum('bhncs,bhnsv->bhncv', scores, v)
    xi = jnp.exp((idx + 1.0) * log_gamma[:, None])
    zeta = jnp.exp((CHUNK - 1.0 - idx) * log_gamma[:, None])
    g_chunk = jnp.exp(CHUNK * log_gamma)
    kz = k * zeta[:, None, :, None]

    def step(state, inp):
        qc, kc, vc = inp
        out = jnp.einsum('bhck,bhkv->bhcv', qc, state) * xi[:, :, None]
        state = state * g_chunk[:, None, None] + jnp.einsum('bhck,bhcv->bhkv', kc, vc)
        return state, out

    s0 = jnp.zeros((bsz, nh, dk, dv), jnp.float32)
    _, cross = lax.scan(step, s0, (jnp.moveaxis(q, 2, 0), jnp.moveaxis(kz, 2, 0), jnp.moveaxis(v, 2, 0)))
    return _from_chunks(jnp.moveaxis(cross, 0, 2) + inner)

def _rg_lru(x, w_a, b_a, w_x, b_x, lam):
    bsz, seq, width = x.shape
    xb = x.reshape(bsz, seq, LRU_BLOCKS, LRU_BLOCK)
    r = jax.nn.sigmoid(jnp.einsum('btnc,ncd->btnd', xb, w_a) + b_a).reshape(bsz, seq, width)
    i = jax.nn.sigmoid(jnp.einsum('btnc,ncd->btnd', xb, w_x) + b_x).reshape(bsz, seq, width)
    log_a = -LRU_C * r * jax.nn.softplus(-lam)
    a = jnp.exp(log_a)
    b = jnp.sqrt(-jnp.expm1(2.0 * log_a)) * (i * x)

    def combine(left, right):
        a1, b1 = left
        a2, b2 = right
        return a1 * a2, a2 * b1 + b2

    _, h = lax.associative_scan(combine, (a, b), axis=1)
    return h

def _hybrid_mixer(h, positions, log_gamma, w_in, dn_conv_w, dn_a_log, dn_dt_bias, dn_norm_w,
                  lru_conv_w, lru_conv_b, lru_wa, lru_ba, lru_wx, lru_bx, lru_lambda, w_branch, w_out):
    bsz, seq, _ = h.shape
    f32 = jnp.float32
    u = h @ w_in
    split_points = [int(p) for p in np.cumsum(IN_SIZES)[:-1]]
    (a_qkv, a_alpha, a_beta, a_z, b_q, b_k, b_v, b_g, c_x, c_g, gate_logits) = jnp.split(u, split_points, axis=-1)

    a_qkv = jax.nn.silu(_causal_dwconv(a_qkv, dn_conv_w)).astype(f32)
    qa, ka, va = jnp.split(a_qkv, [DN_QK, 2 * DN_QK], axis=-1)
    qa = qa.reshape(bsz, seq, DN_HEADS, DN_DK)
    ka = ka.reshape(bsz, seq, DN_HEADS, DN_DK)
    va = va.reshape(bsz, seq, DN_HEADS, DN_DV)
    g_a = -jnp.exp(dn_a_log.astype(f32)) * jax.nn.softplus(a_alpha.astype(f32) + dn_dt_bias.astype(f32))
    beta_a = jax.nn.sigmoid(a_beta.astype(f32))
    oa = _gated_delta_rule(qa, ka, va, g_a, beta_a)
    z_a = a_z.astype(f32).reshape(bsz, seq, DN_HEADS, DN_DV)
    oa = _head_rms(oa) * dn_norm_w.astype(f32) * jax.nn.silu(z_a)
    y_a = oa.reshape(bsz, seq, DN_VW).astype(h.dtype)

    qb = _rotary(b_q.astype(f32).reshape(bsz, seq, RET_HEADS, RET_DK), positions)
    kb = _rotary(b_k.astype(f32).reshape(bsz, seq, RET_HEADS, RET_DK), positions)
    vb = b_v.astype(f32).reshape(bsz, seq, RET_HEADS, RET_DV)
    ob = _retention(qb, kb, vb, log_gamma)
    ob = _head_groupnorm(ob) * jax.nn.silu(b_g.astype(f32).reshape(bsz, seq, RET_HEADS, RET_DV))
    y_b = ob.reshape(bsz, seq, RET_VW).astype(h.dtype)

    xc = _causal_dwconv(c_x, lru_conv_w, lru_conv_b).astype(f32)
    hc = _rg_lru(xc, lru_wa.astype(f32), lru_ba.astype(f32), lru_wx.astype(f32), lru_bx.astype(f32), lru_lambda.astype(f32))
    y_c = (hc * jax.nn.gelu(c_g.astype(f32))).astype(h.dtype)

    ys = jnp.stack([y_a, y_b, y_c], axis=2)
    branch = jnp.einsum('btnw,nwd->btnd', ys, w_branch)
    gates = jax.nn.sigmoid(gate_logits.reshape(bsz, seq, N_BRANCH, D_MODEL))
    merged = jnp.sum(gates * branch, axis=2)
    return merged @ w_out

def _conv_ffn(h, w_up, conv_w, conv_b, w_down):
    up = _causal_dwconv(h @ w_up, conv_w, conv_b)
    gate, val = jnp.split(up, 2, axis=-1)
    return (jax.nn.silu(gate) * val) @ w_down

def setup_inputs(seed: int = 0) -> dict:
    key = jax.random.key(seed)
    ks = jax.random.split(key, 24)
    f32 = jnp.float32

    def nrm(k, shape, scale):
        return jax.random.normal(k, shape, f32) * scale

    x = nrm(ks[0], (BATCH, SEQ, D_MODEL), 1.0)
    offsets = jax.random.randint(ks[1], (BATCH, 1), 0, 4096, dtype=jnp.int32)
    positions = offsets + jnp.arange(SEQ, dtype=jnp.int32)[None, :]
    attn_norm = 1.0 + nrm(ks[2], (DEPTH, D_MODEL), 0.02)
    w_in = nrm(ks[3], (DEPTH, D_MODEL, N_IN), D_MODEL ** -0.5)
    dn_conv_w = nrm(ks[4], (DEPTH, DN_CONV, DN_QKV), DN_CONV ** -0.5)
    dn_a_log = jnp.log(jax.random.uniform(ks[5], (DEPTH, DN_HEADS), f32, 1.0, 16.0))
    dt = jnp.exp(jax.random.uniform(ks[6], (DEPTH, DN_HEADS), f32, math.log(0.001), math.log(0.1)))
    dn_dt_bias = dt + jnp.log(-jnp.expm1(-dt))
    dn_norm_w = 1.0 + nrm(ks[7], (DEPTH, DN_DV), 0.02)
    lru_conv_w = nrm(ks[8], (DEPTH, LRU_CONV, LRU_WIDTH), LRU_CONV ** -0.5)
    lru_conv_b = nrm(ks[9], (DEPTH, LRU_WIDTH), 0.01)
    lru_wa = nrm(ks[10], (DEPTH, LRU_BLOCKS, LRU_BLOCK, LRU_BLOCK), LRU_BLOCK ** -0.5)
    lru_ba = nrm(ks[11], (DEPTH, LRU_BLOCKS, LRU_BLOCK), 0.01)
    lru_wx = nrm(ks[12], (DEPTH, LRU_BLOCKS, LRU_BLOCK, LRU_BLOCK), LRU_BLOCK ** -0.5)
    lru_bx = nrm(ks[13], (DEPTH, LRU_BLOCKS, LRU_BLOCK), 0.01)
    a0 = jax.random.uniform(ks[14], (DEPTH, LRU_WIDTH), f32, 0.9, 0.999) ** (1.0 / LRU_C)
    lru_lambda = jnp.log(a0) - jnp.log1p(-a0)
    w_branch = nrm(ks[15], (DEPTH, N_BRANCH, BRANCH_WIDTH, D_MODEL), BRANCH_WIDTH ** -0.5)
    w_out = nrm(ks[16], (DEPTH, D_MODEL, D_MODEL), D_MODEL ** -0.5)
    ffn_norm = 1.0 + nrm(ks[17], (DEPTH, D_MODEL), 0.02)
    w_up = nrm(ks[18], (DEPTH, D_MODEL, 2 * D_FF), D_MODEL ** -0.5)
    ffn_conv_w = nrm(ks[19], (DEPTH, FFN_CONV, 2 * D_FF), FFN_CONV ** -0.5)
    ffn_conv_b = nrm(ks[20], (DEPTH, 2 * D_FF), 0.01)
    w_down = nrm(ks[21], (DEPTH, D_FF, D_MODEL), D_FF ** -0.5)
    final_norm = 1.0 + nrm(ks[22], (D_MODEL,), 0.02)
    return {'x': x, 'positions': positions, 'attn_norm': attn_norm, 'w_in': w_in, 'dn_conv_w': dn_conv_w,
            'dn_a_log': dn_a_log, 'dn_dt_bias': dn_dt_bias, 'dn_norm_w': dn_norm_w, 'lru_conv_w': lru_conv_w,
            'lru_conv_b': lru_conv_b, 'lru_wa': lru_wa, 'lru_ba': lru_ba, 'lru_wx': lru_wx, 'lru_bx': lru_bx,
            'lru_lambda': lru_lambda, 'w_branch': w_branch, 'w_out': w_out, 'ffn_norm': ffn_norm, 'w_up': w_up,
            'ffn_conv_w': ffn_conv_w, 'ffn_conv_b': ffn_conv_b, 'w_down': w_down, 'final_norm': final_norm}

def reference(x, positions, attn_norm, w_in, dn_conv_w, dn_a_log, dn_dt_bias, dn_norm_w, lru_conv_w, lru_conv_b,
              lru_wa, lru_ba, lru_wx, lru_bx, lru_lambda, w_branch, w_out, ffn_norm, w_up, ffn_conv_w, ffn_conv_b,
              w_down, final_norm):
    log_gamma = jnp.log(1.0 - 2.0 ** (-5.0 - jnp.arange(RET_HEADS, dtype=jnp.float32)))
    for layer in range(DEPTH):
        h = _rms_norm(x, attn_norm[layer])
        x = x + _hybrid_mixer(h, positions, log_gamma, w_in[layer], dn_conv_w[layer], dn_a_log[layer],
                              dn_dt_bias[layer], dn_norm_w[layer], lru_conv_w[layer], lru_conv_b[layer],
                              lru_wa[layer], lru_ba[layer], lru_wx[layer], lru_bx[layer], lru_lambda[layer],
                              w_branch[layer], w_out[layer])
        h = _rms_norm(x, ffn_norm[layer])
        x = x + _conv_ffn(h, w_up[layer], ffn_conv_w[layer], ffn_conv_b[layer], w_down[layer])
    return _rms_norm(x, final_norm)


_drawn_inputs = setup_inputs


def setup_inputs(seed=0):
    import zlib

    import numpy as np

    out = dict(_drawn_inputs(seed))
    spreads = {}
    factors = {'dn_norm_w': 5.793,
     'lru_ba': 64.0,
     'lru_bx': 64.0,
     'ffn_norm': 2.726,
     'ffn_conv_b': 5.379,
     'final_norm': 7.99,
     'lru_conv_b': 3.934}
    for name, (base, spread) in spreads.items():
        noise = np.random.default_rng([zlib.crc32(name.encode()), seed]).standard_normal(out[name].shape)
        drawn = base * np.exp(spread * noise) if base else spread * noise
        out[name] = jnp.asarray(drawn.astype(out[name].dtype))
    for name, factor in factors.items():
        out[name] = (out[name] * factor).astype(out[name].dtype)
    return out
```

```python
from contextlib import ExitStack

import concourse.bass as bass
from concourse import mybir

F32 = mybir.dt.float32
F32R = mybir.dt.float32r
I32 = mybir.dt.int32
ACT = mybir.ActivationFunctionType
ALU = mybir.AluOpType
MUL, ADD, SUB, MAX, MIN = ALU.mult, ALU.add, ALU.subtract, ALU.max, ALU.min

P = 128
T = 512
D = 1024
KT = D // P
L = 2
NC = T // P
NH = 4
EPS = 1e-6
NLV = 6
DT_ = 8

U_QKV, U_CX, U_Z, U_BQK, U_CG, U_BV, U_BG = 0, 12, 16, 20, 24, 28, 32
U_MIX = 36
U_OUT = U_MIX + 4 * DT_
U_FFN = (U_OUT + DT_, U_OUT + DT_ + 24 + DT_)
PAIRS = (12, 10)
U_DOWN = (U_FFN[0] + 24, U_FFN[1] + 20)
NU = U_DOWN[1] + DT_
SLOT = 12 * P
NST = 4
NBK = NU // 4
START = 1

C_ID, C_ONE, C_U, C_PERM, C_M1T = 0, P, 2 * P, 3 * P, 4 * P
C_NEG = 5 * P
C_Z15 = C_NEG + 7 * P
C_MISC = C_Z15 + 16
C_DM = C_MISC + 4
NCONST = C_DM + NH * T
M_GA, M_GF, M_CW, M_NW, M_LW, M_LB, M_BA, M_BX = 0, 8, 16, 64, 65, 81, 85, 89
M_LAM, M_DT, M_ALOG, M_WAB = 93, 97, 101, 105
M_WA = M_WAB + 64
M_WX = M_WA + 512
NMP = M_WX + 512 + 7
F_W, F_B = 0, 132
NFP = 176


def unit_k(u):
    if u >= U_MIX and u < U_OUT:
        return 12 if (u - U_MIX) % 4 == 3 else 8
    if U_DOWN[0] <= u < U_DOWN[0] + 8:
        return 12
    if u >= U_DOWN[1]:
        return 10
    return 8


def build(nc, consts, posd, x_in, wst, mpd, fpd, fnd, out):
    with ExitStack() as ctx:
        base = -(-nc.sbuf_base // 64) * 64
        place = {"at": base}

        def sb(name, shape, dt=F32, at=None):
            n = 4
            for s in shape[1:]:
                n *= s
            off = place["at"] if at is None else at
            if at is None:
                place["at"] += -(-n // 32) * 32
            return nc.alloc_sbuf_tensor_at(name, shape, dt, offset=off)

        X = sb("x_res", [P, KT, T])
        H = sb("h_parts", [P, KT, 2, T], F32R)
        STG = sb("w_stage", [P, NST, SLOT])
        SPL = sb("w_parts", [P, 2, 2, SLOT], F32R)
        y_at = place["at"]
        Y = sb("y_parts", [P, 12, 2, T], F32R)
        CO = sb("consts", [P, NCONST])
        CS = sb("cos_sin", [P, 2, T])
        MP = sb("mixer_params", [P, NMP])
        FP = sb("ffn_params", [P, NFP])
        FN = sb("final_norm", [P, 8])
        WAB = sb("ab_parts", [P, 2, 8, 8], F32R)
        SM = sb("small", [P, 480])
        left_at = place["at"]
        KK = [sb(f"area{i}", [P, 4, T]) for i in range(5)]
        TM = [sb(f"tmp{i}", [P, T]) for i in range(6)]
        assert place["at"] <= nc.sbuf_usable_end, (place["at"], nc.sbuf_usable_end)

        VT = sb("dn_vT", [P, 4, T], at=y_at)
        ST = sb("dn_state", [P, T], at=y_at)
        RR = sb("dn_r", [P, T], at=y_at + 2048)
        VN = sb("dn_vnew", [P, T], at=y_at + 4096)
        EG = sb("dn_eg", [P, 2, T], at=y_at + 8192)
        YM = sb("dn_ym", [P, 2, T], at=y_at + 8192)
        EL = sb("dn_el", [P, 2, T], at=y_at + 12288)
        DTT = sb("dn_tT", [P, NC, T], at=y_at + 16384)
        OT = sb("dn_out", [P, 4, T], at=y_at + 24576)
        DD = sb("dn_t", [P, NC, T], at=y_at + 32768)
        LT = sb("dn_lT", [P, NC, T], at=y_at + 40960)
        ZS = sb("z_silu", [P, 4, T], at=y_at + 32768)
        BGS = sb("bg_silu", [P, 4, T], at=y_at + 16384)
        RAW = sb("ret_raw", [P, 4, T], at=y_at + 16384)
        XC = sb("lru_x", [P, 4, T], at=y_at + 40960)
        KTT, QTT, ATT, VB, KD = KK
        RQ, BV, OB = KK[0], KK[1], KK[4]
        SC = [sb(f"ret_sc{i}", [P, 1280], at=left_at + 16384 + 5120 * i) for i in range(2)]
        TI, TH, INV = KK[2], KK[3], KK[4]
        MM = sb("merged", [P, 8, T], at=left_at)
        GT = sb("gates", [P, 2, 4, T], at=left_at + 16384)
        SQN = KK[4]
        HN = sb("normed", [P, KT, T], at=left_at)
        CG, TG, CV, SQ = KK[0], KK[1], KK[2], [TM[2], TM[3]]

        bank = [ctx.enter_context(nc.psum_tensor(f"bank{i}", [P, T], F32)) for i in range(8)]

        sems = {}

        def sem(name, per_layer=0):
            s = ctx.enter_context(nc.semaphore(name))
            sems[name] = per_layer
            return s

        ld_const, ld_x, ld_pos, ld_mp, ld_fp = (sem(n) for n in ("ld_const", "ld_x", "ld_pos", "ld_mp", "ld_fp"))
        ld_w = [sem(f"ld_w{i}") for i in range(NST)]
        w_hi, w_lo, gemm_done = sem("w_hi"), sem("w_lo"), sem("gemm_done")
        bank_free = [sem(f"bank_free{i}") for i in range(4)]
        rot_v, rot_a = sem("rot_v"), sem("rot_a")
        sq_ready, norm_mm, rs_done, ri_done = sem("sq_ready"), sem("norm_mm"), sem("rs_done"), sem("ri_done")
        hn_ready, h_hi = sem("hn_ready"), sem("h_hi")
        h_lo = (sem("h_lo_even"), sem("h_lo_odd"))
        wab_hi, wab_lo, ab_done = sem("wab_hi"), sem("wab_lo"), sem("ab_done")
        sm_v, sm_a, gc_done = sem("sm_v"), sem("sm_a"), sem("gc_done")
        cv_ready, cv_acc, th_ready, silu_done = sem("cv_ready"), sem("cv_acc"), sem("th_ready"), sem("silu_done")
        rn_sq, rn_mm, rn_rs, rn_ri, rn_b, rn_app = (sem("rn_" + n) for n in ("sq", "mm", "rs", "ri", "b", "app"))
        ug_ready, grow_done, eg_ready, el_pre, el_ready = (
            sem(n) for n in ("ug_ready", "grow_done", "eg_ready", "el_pre", "el_ready"))
        kk_done, qk_done, l_ready, at_ready, qd_ready = (
            sem(n) for n in ("kk_done", "qk_done", "l_ready", "at_ready", "qd_ready"))
        tv_done, tk_done, tl_done, ta_done = (sem(n) for n in ("tv_done", "tk_done", "tl_done", "ta_done"))
        vb_ready, kd_ready, lt_ready, att_ready = (sem(n) for n in ("vb_ready", "kd_ready", "lt_ready", "att_ready"))
        d_pre, d_init, dt_pre, dt_init = (sem(n) for n in ("d_pre", "d_init", "dt_pre", "dt_init"))
        y_done, ym_ready, p_done, t_done, d_upd, dt_upd, dt_fin = (
            sem(n) for n in ("y_done", "ym_ready", "p_done", "t_done", "d_upd", "dt_upd", "dt_fin"))
        ks_done, r_ready, vn_done, vn_ready, o_done, o_ready, su_done, s_upd = (
            sem(n) for n in ("ks_done", "r_ready", "vn_done", "vn_ready", "o_done", "o_ready", "su_done", "s_upd"))
        zt_ready, ya_v, y_fin, y_hi, y_lo = sem("zt_ready"), sem("ya_v"), sem("y_fin"), sem("y_hi"), sem("y_lo")
        raw_ready, perm_done, rot_m1, rot_m2, rq_ready = (
            sem(n) for n in ("raw_ready", "perm_done", "rot_m1", "rot_m2", "rq_ready"))
        bvt_done, bv_ready, sc_done, sc_ready, pv_done, ob_ready = (
            sem(n) for n in ("bvt_done", "bv_ready", "sc_done", "sc_ready", "pv_done", "ob_ready"))
        mean_done, cen_ready = sem("mean_done"), sem("cen_ready")
        xc_ready, lru_acc, lru_mm, lru_t, lru_th, lru_sq, lru_v = (
            sem(n) for n in ("xc_ready", "lru_acc", "lru_mm", "lru_t", "lru_th", "lru_sq", "lru_v"))
        bg_ready = sem("bg_ready")
        ge_a, ge_t, ge_v, mg_v, mg_done = (sem(n) for n in ("ge_a", "ge_t", "ge_v", "mg_v", "mg_done"))
        fc_ready, fc_acc, ft_ready, fg_v, fg_done, f_hi, f_lo = (
            sem(n) for n in ("fc_ready", "fc_acc", "ft_ready", "fg_v", "fg_done", "f_hi", "f_lo"))
        out_ready, stored, ld_dm = sem("out_ready"), sem("stored"), sem("ld_dm")

        block = ctx.enter_context(nc.Block())

        ident, ones, upper, perm = (CO[:, c:c + P] for c in (C_ID, C_ONE, C_U, C_PERM))
        neg_m1t = CO[:, C_M1T:C_M1T + P]
        eps_col = CO[:, C_MISC + 3:C_MISC + 4]

        def neg_mask(lv):
            return CO[:, C_NEG + lv * P:C_NEG + (lv + 1) * P]

        def over_heads(m):
            return m.unsqueeze(1).to_broadcast([P, NH, P])

        def heads(t):
            return t.rearrange("p (h n) -> p h n", h=NH)

        def col(t, i):
            return t[:, i:i + 1]

        def chunk(c):
            return slice(c * P, (c + 1) * P)

        def pb(c, role):
            return bank[(4 if c % 2 == 0 else 0) + role][:, :]

        def lru_bank(j):
            return 4 + (j % 2) * 2

        n_sm = [0]

        def small(n):
            n_sm[0] += n
            assert n_sm[0] <= 480
            return SM[:, n_sm[0] - n:n_sm[0]]

        XS, AX, EX, WM, RC, LW, SP = (small(20) for _ in range(7))
        TB, BE, HB, GG, GCS, DL, EGC, EGT, EKD, NBG = (
            small(16), small(16), small(16), small(16), small(32), small(16), small(16), small(16), small(16), small(16))
        EA, SP2, HBA = small(4), small(4), small(8)
        ROW, ROWI = TM[4], TM[5]

        @block.sync
        def _(sp):
            sp.dma_start(CO[:, 0:C_DM], consts[:, 0:C_DM]).then_inc(ld_const, 16)
            sp.dma_start(X[:, :, :], x_in).then_inc(ld_x, 16)
            sp.dma_start(FN[:, :], fnd).then_inc(ld_x, 16)
            sp.dma_start(TM[0][:, :].bitcast(I32), posd).then_inc(ld_pos, 16)
            with sp.Fori(0, L) as l:
                sp.wait_ge(f_lo, START + l * 22)
                sp.dma_start(MP[:, :], mpd[bass.ds(l, 1), :, :].rearrange("l p n -> (l p) n")).then_inc(ld_mp, 16)
                for u in range(NU):
                    sp.wait_ge(w_lo, START + l * NU + max(u - 3, 0))
                    n = unit_k(u) * P
                    sp.dma_start(STG[:, u % NST, 0:n],
                                 wst[bass.ds(l * NU + u, 1), :, 0:n].rearrange("l p n -> (l p) n"))\
                      .then_inc(ld_w[u % NST], 16)
                    if u == 12:
                        sp.dma_start(CO[:, C_DM:NCONST], consts[:, C_DM:NCONST]).then_inc(ld_dm, 16)
                    if u == 40:
                        sp.dma_start(FP[:, :], fpd[bass.ds(l, 1), :, :].rearrange("l p n -> (l p) n"))\
                          .then_inc(ld_fp, 16)
            for k in range(KT):
                sp.wait_ge(out_ready, k + 1)
                sp.dma_start(out[:, k, :], HN[:, k, :]).then_inc(stored, 16)
            sp.wait_ge(stored, 16 * KT)

        @block.scalar
        def _(act):
            def split_hi(l, u):
                act.wait_ge(ld_w[u % NST], 16 * (l * NBK) + 16 * (u // 4 + 1))
                act.wait_ge(gemm_done, START + l * NU + max(u - 1, 0))
                n = unit_k(u) * P
                act.activation(SPL[:, u % 2, 0, 0:n], STG[:, u % NST, 0:n], ACT.Copy).then_inc(w_hi, 1)

            def next_split(l, u):
                if u + 2 < NU:
                    split_hi(l, u + 2)

            def done(l, u):
                act.wait_ge(gemm_done, START + l * NU + u + 1)

            def norm_rows(l, n):
                for k in range(KT):
                    if n == 1:
                        act.wait_ge(bank_free[k % 4], START + l * NBK + (U_OUT + k) // 4 + 1)
                    if k >= 4:
                        act.wait_ge(norm_mm, l * 16 + n * 8 + k - 3)
                    act.activation(SQN[:, k % 4, :], X[:, k, :], ACT.Square).then_inc(sq_ready, 1)
                act.wait_ge(norm_mm, l * 16 + n * 8 + 8)
                act.activation(ROW[:, :], bank[4][:, :], ACT.Sqrt, scale=1.0 / D, bias=eps_col).then_inc(rs_done, 1)

            def h_split(l, n0, src):
                for k in range(KT):
                    act.wait_ge(hn_ready, l * 24 + n0 + k + 1)
                    act.activation(H[:, k, 0, :], src(k), ACT.Copy).then_inc(h_hi, 1)

            def square(l, b0, j, src, buf):
                if j >= 2:
                    act.wait_ge(rn_mm, l * 16 + b0 + j - 1)
                act.activation(buf, src, ACT.Square).then_inc(rn_sq, 1)

            def rows_root(l, b0, n):
                act.wait_ge(rn_mm, l * 16 + b0 + n)
                if n == 8:
                    act.activation(ROW[0:8, :], bank[4][0:8, :], ACT.Sqrt, scale=CO[0:8, C_MISC + 1:C_MISC + 2],
                                   bias=CO[0:8, C_MISC + 2:C_MISC + 3]).then_inc(rn_rs, 1)
                else:
                    act.activation(ROW[0:n, :], bank[4][0:n, :], ACT.Sqrt, scale=1.0 / P,
                                   bias=eps_col[0:n, :]).then_inc(rn_rs, 1)

            act.wait_ge(rot_v, 13)
            act.activation(CS[:, 1, :], TM[1][:, :], ACT.Sin).then_inc(rot_a, 1)
            act.activation(TM[2][:, :], TM[1][:, :], ACT.Sin, scale=0.5).then_inc(rot_a, 1)
            act.wait_ge(ld_x, 32)
            with act.Fori(0, L) as l:
                split_hi(l, 0)
                split_hi(l, 1)
                norm_rows(l, 0)
                act.wait_ge(ld_mp, l * 16 + 16)
                act.activation(WAB[:, 0, :, :].rearrange("p a b -> p (a b)"), MP[:, M_WAB:M_WAB + 64],
                               ACT.Copy).then_inc(wab_hi, 1)
                h_split(l, 0, lambda k: HN[:, k, :])
                next_split(l, 0)

                ab = bank[5][:, 0:32].rearrange("p (c n) -> p c n", n=8)
                act.wait_ge(ab_done, l + 1)
                act.activation(TB.rearrange("p (c h) -> p c h", h=4), ab[:, :, 4:8], ACT.Tanh, scale=0.5)\
                   .then_inc(sm_a, 1)
                act.activation(EA, MP[:, M_ALOG:M_ALOG + 4], ACT.Exp).then_inc(sm_a, 1)
                act.wait_ge(sm_v, l * 17 + 3)
                act.activation(EX, AX, ACT.Exp, scale=-1.0).then_inc(sm_a, 1)
                act.wait_ge(sm_a, l * 7 + 3)
                act.activation(LW, EX, ACT.Ln, bias=CO[:, C_ONE:C_ONE + 1]).then_inc(sm_a, 1)
                act.wait_ge(sm_v, l * 17 + 15)
                act.activation(EGC, GCS[:, 0:16], ACT.Exp).then_inc(sm_a, 1)
                act.activation(EGT, GCS[:, 16:32], ACT.Exp).then_inc(sm_a, 1)
                act.wait_ge(sm_v, l * 17 + 16)
                act.activation(EKD, DL, ACT.Exp).then_inc(sm_a, 1)

                def qk_square(j):
                    act.wait_ge(silu_done, l * 12 + j + 1)
                    square(l, 0, j, QTT[:, j, :] if j < 4 else KTT[:, j - 4, :], EL[:, j % 2, :])

                for u in range(12):
                    if u >= 1:
                        next_split(l, u)
                    done(l, u)
                    if u >= 2:
                        act.wait_ge(silu_done, l * 12 + u - 1)
                    act.activation(TM[u % 2][:, :], bank[u % 4][:, :], ACT.Identity,
                                   scale=col(MP, M_CW + u * 4 + 3)).then_inc(cv_ready, 1)
                    if 1 <= u < 9:
                        qk_square(u - 1)
                    act.wait_ge(bank_free[u % 4], START + l * NBK + u // 4 + 1)
                    act.activation(TM[2 + u % 2][:, :], TM[u % 2][:, :], ACT.Tanh, scale=0.5).then_inc(th_ready, 1)
                    if u == 9:
                        rows_root(l, 0, 8)

                def prep_1(c):
                    i = l * NC + c
                    act.wait_ge(grow_done, i + 1)
                    if c >= 2:
                        act.wait_ge(qd_ready, i - 1)
                    act.activation(EG[:, c % 2, :], pb(c, 1), ACT.Exp).then_inc(eg_ready, 1)
                    act.wait_ge(el_pre, i + 1)
                    act.activation(EL[:, c % 2, :], EL[:, c % 2, :], ACT.Exp, scale=-1.0).then_inc(el_ready, 1)
                    act.wait_ge(tv_done, i + 1)
                    for h in range(NH):
                        last = act.activation(VB[:, c, h * P:(h + 1) * P], pb(c, 0)[:, h * P:(h + 1) * P], ACT.Copy,
                                              scale=col(HB, c * 4 + h))
                    last.then_inc(vb_ready, 1)

                def prep_2(c):
                    i = l * NC + c
                    act.wait_ge(tl_done, i + 1)
                    act.activation(LT[:, c, :], pb(c, 1), ACT.Copy).then_inc(lt_ready, 1)
                    act.wait_ge(tk_done, i + 1)
                    for h in range(NH):
                        last = act.activation(KD[:, c, h * P:(h + 1) * P], pb(c, 0)[:, h * P:(h + 1) * P], ACT.Copy,
                                              scale=col(EKD, c * 4 + h))
                    last.then_inc(kd_ready, 1)

                prep_1(0)
                prep_1(1)
                prep_2(0)
                prep_1(2)
                prep_2(1)
                prep_1(3)
                prep_2(2)
                prep_2(3)

                for n in range(20):
                    act.wait_ge(t_done, l * 20 + n + 1)
                    act.activation(DTT[:, n % 4, :], bank[7][:, :], ACT.Copy).then_inc(dt_upd, 1)

                def silu_tanh(u, nth):
                    done(l, u)
                    if nth >= 2:
                        act.wait_ge(bank_free[(u - 2) % 4], START + l * NBK + (u - 2) // 4 + 1)
                    act.activation(TM[2 + u % 2][:, :], bank[u % 4][:, :], ACT.Tanh, scale=0.5).then_inc(zt_ready, 1)

                def fill(n):
                    u = U_CX + n
                    next_split(l, u)
                    if n < 4:
                        done(l, u)
                        act.activation(XC[:, n, :], bank[u % 4][:, :], ACT.Identity, scale=col(MP, M_LW + n * 4 + 3),
                                       bias=col(MP, M_LB + n)).then_inc(xc_ready, 1)
                    else:
                        silu_tanh(u, n - 4)

                for c in range(NC):
                    i = l * NC + c
                    fill(2 * c)
                    act.wait_ge(vn_done, i + 1)
                    if c >= 1:
                        act.wait_ge(su_done, l * 3 + c)
                    act.activation(VN[:, :], bank[5][:, :], ACT.Copy).then_inc(vn_ready, 1)
                    fill(2 * c + 1)
                    act.wait_ge(o_done, i + 1)
                    act.activation(OT[:, :, chunk(c)], heads(bank[6][:, :]), ACT.Copy).then_inc(o_ready, 1)

                act.wait_ge(bank_free[3], START + l * NBK + 5)
                act.wait_ge(o_ready, l * NC + 4)
                for j in range(4):
                    square(l, 8, j, OT[:, j, :], SQ[j % 2][:, :])
                rows_root(l, 8, 4)

                def y_split(nth, t, src):
                    act.wait_ge(y_fin, l * 12 + nth + 1)
                    act.activation(Y[:, t, 0, :], src, ACT.Copy).then_inc(y_hi, 1)

                for i in range(4):
                    u = U_BQK + i
                    next_split(l, u)
                    done(l, u)
                    act.activation(RAW[:, i, :], bank[u % 4][:, :], ACT.Copy).then_inc(raw_ready, 1)
                    act.wait_ge(lru_mm, l * 4 + i + 1)
                    act.activation(TH[:, i, :], bank[lru_bank(i)][:, :], ACT.Tanh, scale=0.5, bias=col(HBA, i))
                    act.activation(TI[:, i, :], bank[lru_bank(i) + 1][:, :], ACT.Tanh, scale=0.5,
                                   bias=col(HBA, 4 + i)).then_inc(lru_t, 1)
                next_split(l, U_CG)
                for j in range(4):
                    act.wait_ge(lru_t, l * 4 + j + 1)
                    act.activation(TH[:, j, :], TH[:, j, :], ACT.Tanh, scale=col(SP2, j), bias=col(SP2, j))\
                       .then_inc(lru_th, 1)
                for i in range(4):
                    y_split(i, i, OT[:, i, :])
                for j in range(4):
                    act.wait_ge(lru_v, l * 28 + j + 1)
                    act.activation(TH[:, j, :], TH[:, j, :], ACT.Sqrt).then_inc(lru_sq, 1)

                def gelu_1(j):
                    u = U_CG + j
                    if j >= 1:
                        next_split(l, u)
                    done(l, u)
                    if j >= 2:
                        act.wait_ge(y_fin, l * 12 + 4 + j - 1)
                    else:
                        act.wait_ge(rq_ready, l * 4 + 4)
                    act.activation(TM[j % 2][:, :], bank[u % 4][:, :], ACT.Square).then_inc(ge_a, 1)

                def gelu_2(j):
                    act.wait_ge(ge_v, l * 8 + 2 * j + 2)
                    act.activation(TM[j % 2][:, :], TM[j % 2][:, :], ACT.Tanh, scale=0.7978845608028654)\
                       .then_inc(ge_t, 1)

                gelu_1(0)
                gelu_1(1)
                gelu_2(0)
                for j in range(4):
                    y_split(4 + j, 8 + j, TM[4 + j % 2][:, :])
                    if j + 2 < 4:
                        gelu_1(j + 2)
                    if j + 1 < 4:
                        gelu_2(j + 1)

                def bv_out(h):
                    act.wait_ge(bvt_done, l * 4 + h + 1)
                    act.activation(BV[:, h, :], bank[4 + h % 2][:, :], ACT.Copy).then_inc(bv_ready, 1)

                for h in range(NH):
                    u = U_BV + h
                    next_split(l, u)
                    done(l, u)
                    act.wait_ge(perm_done, l * 4 + 4)
                    act.activation(RAW[:, h, :], bank[u % 4][:, :], ACT.Copy).then_inc(bank_free[u % 4], 1)
                    if h >= 2:
                        bv_out(h - 2)

                def bg_tanh(h):
                    next_split(l, U_BG + h)
                    silu_tanh(U_BG + h, h)

                bg_tanh(0)
                bv_out(2)
                bv_out(3)

                def retention_out(h):
                    act.wait_ge(pv_done, l * 4 + h + 1)
                    act.activation(OB[:, h, :], bank[7][:, :], ACT.Copy).then_inc(ob_ready, 1)

                bg_tanh(1)
                bg_tanh(2)
                retention_out(0)
                bg_tanh(3)
                for h in range(1, NH):
                    retention_out(h)

                act.wait_ge(bg_ready, l * 4 + 4)
                for j in range(4):
                    act.wait_ge(cen_ready, l * 4 + j + 1)
                    square(l, 12, j, OB[:, j, :], SQ[j % 2][:, :])

                for d in range(DT_):
                    for n in range(4):
                        u = U_MIX + 4 * d + n
                        next_split(l, u)
                        if n < 3:
                            done(l, u)
                            if d >= 2:
                                act.wait_ge(mg_done, l * 8 + d - 1)
                            act.activation(GT[:, d % 2, n, :], bank[n][:, :], ACT.Tanh, scale=0.5)\
                               .then_inc(bank_free[n], 1)
                        if d == 0 and n == 0:
                            rows_root(l, 12, 4)
                        if d == 0 and n == 2:
                            act.wait_ge(y_fin, l * 12 + 12)
                            for h in range(4):
                                y_split(8 + h, 4 + h, OB[:, h, :])
                act.wait_ge(gemm_done, START + l * NU + U_OUT)
                h_split(l, 8, lambda k: MM[:, k, :])
                for d in range(DT_):
                    next_split(l, U_OUT + d)
                norm_rows(l, 1)
                h_split(l, 16, lambda k: HN[:, k, :])

                act.wait_ge(ld_fp, l * 16 + 16)
                p0 = 0
                for g in range(2):
                    for i in range(PAIRS[g]):
                        p, u = p0 + i, U_FFN[g] + 2 * i
                        next_split(l, u)
                        done(l, u)
                        if p >= 2:
                            act.wait_ge(fg_done, l * 22 + p - 1)
                        act.activation(CG[:, p % 2, :], bank[u % 4][:, :], ACT.Identity, scale=col(FP, F_W + p * 3 + 2),
                                       bias=col(FP, F_B + p)).then_inc(fc_ready, 1)
                        act.wait_ge(bank_free[u % 4], START + l * NBK + u // 4 + 1)
                        act.activation(TG[:, p % 2, :], CG[:, p % 2, :], ACT.Tanh, scale=0.5).then_inc(ft_ready, 1)
                        next_split(l, u + 1)
                        done(l, u + 1)
                        if p >= 2:
                            act.wait_ge(f_lo, START + l * 22 + p - 1)
                        act.activation(CV[:, p % 2, :], bank[(u + 1) % 4][:, :], ACT.Identity,
                                       scale=col(FP, F_W + (22 + p) * 3 + 2), bias=col(FP, F_B + 22 + p))\
                           .then_inc(fc_ready, 1)
                        act.wait_ge(fg_done, l * 22 + p + 1)
                        act.activation(Y[:, i, 0, :], CV[:, p % 2, :], ACT.Copy).then_inc(f_hi, 1)
                    for d in range(DT_):
                        next_split(l, U_DOWN[g] + d)
                    p0 += PAIRS[g]
                for b in range(4):
                    act.wait_ge(bank_free[b], START + l * NBK + NBK)
            norm_rows(L, 0)

        @block.gpsimd
        def _(pool):
            def split_lo(l, u):
                pool.wait_ge(w_hi, l * NU + u + 1)
                n = unit_k(u) * P
                pool.tensor_tensor(SPL[:, u % 2, 1, 0:n], STG[:, u % NST, 0:n], SPL[:, u % 2, 0, 0:n], SUB)\
                    .then_inc(w_lo, 1)

            def h_rest(l, batch, src):
                for k in range(1, KT, 2):
                    pool.wait_ge(h_hi, l * 24 + 8 * batch + k + 1)
                    pool.tensor_tensor(H[:, k, 1, :], src[:, k, :], H[:, k, 0, :], SUB).then_inc(h_lo[1], 1)

            pool.memset(SM[:, 470:471], 0.0).then_inc(w_lo, 1)
            with pool.Fori(0, L) as l:
                split_lo(l, 0)
                split_lo(l, 1)
                pool.wait_ge(wab_hi, l + 1)
                pool.tensor_tensor(WAB[:, 1, :, :].rearrange("p a b -> p (a b)"), MP[:, M_WAB:M_WAB + 64],
                                   WAB[:, 0, :, :].rearrange("p a b -> p (a b)"), SUB).then_inc(wab_lo, 1)
                h_rest(l, 0, HN)
                for u in range(2, 14):
                    split_lo(l, u)
                for c in range(NC):
                    i = l * NC + c
                    pool.wait_ge(eg_ready, i + 1)
                    pool.wait_ge(qk_done, i + 1)
                    pool.tensor_tensor(QTT[:, :, chunk(c)], QTT[:, :, chunk(c)], heads(EG[:, c % 2, :]), MUL)\
                        .then_inc(qd_ready, 1)
                    pool.wait_ge(lt_ready, i + 1)
                    pool.tensor_tensor(heads(DTT[:, c, :]), heads(LT[:, c, :]), over_heads(neg_m1t), MUL)\
                        .then_inc(dt_pre, 1)
                    pool.wait_ge(dt_pre, i + 1)
                    pool.tensor_tensor(heads(DTT[:, c, :]), heads(DTT[:, c, :]), over_heads(ident), ADD)\
                        .then_inc(dt_init, 1)
                for u in range(14, NU):
                    split_lo(l, u)
                    if u == U_OUT + 1:
                        h_rest(l, 1, MM)
                    if u == U_FFN[0] + 1:
                        h_rest(l, 2, HN)

        @block.tensor
        def _(pe):
            def product(l, u, dst, k0, src, nk=None, last_signal=True, arrives=None):
                nk = unit_k(u) if nk is None else nk
                for k in range(nk):
                    if arrives is not None:
                        arrives(k)
                    w = [SPL[:, u % 2, part, (k0 + k) * P:(k0 + k + 1) * P] for part in range(2)]
                    for n, (a, b) in enumerate(((0, 0), (0, 1), (1, 0))):
                        mm = pe.matmul(dst, w[a], src(k0 + k)[:, b, :], start=(k == 0 and n == 0),
                                       stop=(k == nk - 1 and n == 2))
                if last_signal:
                    mm.then_inc(gemm_done, 1)

            def h_part(k):
                return H[:, k, :, :]

            def y_part(k):
                return Y[:, k, :, :]

            def gemm(l, u, src=h_part, arrives=None):
                pe.wait_ge(w_lo, START + l * NU + u + 1)
                pe.wait_ge(bank_free[u % 4], START + l * NBK + u // 4)
                product(l, u, bank[u % 4][:, :], 0, src, arrives=arrives)

            def h_arrives(l, batch):
                return lambda k: pe.wait_ge(h_lo[k % 2], l * 12 + 4 * batch + k // 2 + 1)

            def norm_sums(l, n):
                for k in range(KT):
                    pe.wait_ge(sq_ready, l * 16 + n * 8 + k + 1)
                    pe.matmul(bank[4][:, :], ones, SQN[:, k % 4, :], start=(k == 0), stop=(k == KT - 1))\
                      .then_inc(norm_mm, 1)

            def row_sum(l, b0, j, n, buf):
                pe.wait_ge(rn_sq, l * 16 + b0 + j + 1)
                pe.matmul(bank[4][0:n, :], CO[:, C_Z15 + 7 - j:C_Z15 + 7 - j + n], buf,
                          start=(j == 0), stop=(j == n - 1)).then_inc(rn_mm, 1)

            def row_broadcast(l, b0, n, nth):
                pe.wait_ge(rn_ri, l * 3 + nth + 1)
                for j in range(n):
                    if j >= 2:
                        pe.wait_ge(rn_app, l * 16 + b0 + j - 1)
                    pe.matmul(bank[6 + j % 2][:, :], CO[0:n, C_ID + j:C_ID + j + 1].to_broadcast([n, P]),
                              ROWI[0:n, :], start=True, stop=True).then_inc(rn_b, 1)

            pe.wait_ge(ld_const, 16)
            pe.matmul(bank[7][:, 0:2], ident, ident[:, 0:2], start=True, stop=True).then_inc(gemm_done, 1)
            with pe.Fori(0, L) as l:
                norm_sums(l, 0)
                gemm(l, 0, arrives=h_arrives(l, 0))
                pe.wait_ge(wab_lo, l + 1)
                for c in range(NC):
                    for k in range(KT):
                        for n, (a, b) in enumerate(((0, 0), (1, 0), (0, 1))):
                            mm = pe.matmul(bank[5][:, c * 8:c * 8 + 8], H[:, k, a, chunk(c)], WAB[:, b, k, :],
                                           start=(k == 0 and n == 0), stop=(k == KT - 1 and n == 2))
                mm.then_inc(ab_done, 1)
                gemm(l, 1)
                gemm(l, 2)
                pe.wait_ge(sm_v, l * 17 + 14)
                pe.matmul(bank[5][:, 64:80], upper, GG, start=True, stop=True)
                pe.matmul(bank[5][:, 80:96], ones, GG, start=True, stop=True).then_inc(gc_done, 1)
                for u in range(3, 12):
                    gemm(l, u)
                    if u == 3:
                        row_sum(l, 0, 0, 8, EL[:, 0, :])
                    if u - 2 < 8:
                        row_sum(l, 0, u - 2, 8, EL[:, u % 2, :])
                row_broadcast(l, 0, 8, 0)

                def prep_1(c):
                    i = l * NC + c
                    pe.wait_ge(ug_ready, i + 1)
                    if c >= 2:
                        pe.wait_ge(lt_ready, i - 1)
                        pe.wait_ge(att_ready, i - 1)
                        pe.wait_ge(kd_ready, i - 1)
                    if c == 1:
                        pe.wait_ge(silu_done, l * 12 + 12)
                    pe.matmul(pb(c, 1), ones, TM[c % 2][:, :], start=True, stop=True).then_inc(grow_done, 1)
                    if c == 0:
                        pe.wait_ge(rn_app, l * 16 + 8)
                        pe.wait_ge(silu_done, l * 12 + 12)
                    for h in range(NH):
                        k_c = KTT[:, h, chunk(c)]
                        mm = pe.matmul(pb(c, 2)[:, h * P:(h + 1) * P], k_c, k_c, start=True, stop=True)
                    mm.then_inc(kk_done, 1)
                    for h in range(NH):
                        mm = pe.matmul(pb(c, 3)[:, h * P:(h + 1) * P], QTT[:, h, chunk(c)], KTT[:, h, chunk(c)],
                                       start=True, stop=True)
                    mm.then_inc(qk_done, 1)
                    for h in range(NH):
                        mm = pe.transpose(pb(c, 0)[:, h * P:(h + 1) * P], VT[:, h, chunk(c)], ident)
                    mm.then_inc(tv_done, 1)

                def prep_2(c):
                    i = l * NC + c
                    pe.wait_ge(l_ready, i + 1)
                    pe.wait_ge(eg_ready, i + 1)
                    for h in range(NH):
                        mm = pe.transpose(pb(c, 1)[:, h * P:(h + 1) * P], TM[4 + c % 2][:, h * P:(h + 1) * P], ident)
                    mm.then_inc(tl_done, 1)
                    pe.wait_ge(at_ready, i + 1)
                    for h in range(NH):
                        mm = pe.transpose(pb(c, 2)[:, h * P:(h + 1) * P], TM[2 + c % 2][:, h * P:(h + 1) * P], ident)
                    mm.then_inc(ta_done, 1)
                    pe.wait_ge(vb_ready, i + 1)
                    for h in range(NH):
                        mm = pe.transpose(pb(c, 0)[:, h * P:(h + 1) * P], KTT[:, h, chunk(c)], ident)
                    mm.then_inc(tk_done, 1)

                prep_1(0)
                prep_1(1)
                prep_2(0)
                prep_1(2)
                prep_2(1)
                prep_1(3)
                prep_2(2)
                prep_2(3)

                def level_y(n):
                    c = n % 4
                    if n < 4:
                        pe.wait_ge(d_init, l * 4 + c + 1)
                        if n == 0:
                            pe.wait_ge(att_ready, l * 4 + 4)
                            pe.wait_ge(kd_ready, l * 4 + 4)
                            pe.wait_ge(lt_ready, l * 4 + 4)
                    else:
                        pe.wait_ge(d_upd, l * 20 + n - 3)
                    if n >= 2:
                        pe.wait_ge(ym_ready, l * 24 + n - 1)
                    for h in range(NH):
                        s = slice(h * P, (h + 1) * P)
                        mm = pe.matmul(bank[4 + n % 2][:, s], LT[:, c, s], DD[:, c, s], start=True, stop=True)
                    mm.then_inc(y_done, 1)

                def level_t(n):
                    pe.wait_ge(d_upd, l * 20 + n + 1)
                    if n >= 1:
                        pe.wait_ge(dt_upd, l * 20 + n)
                    for h in range(NH):
                        s = slice(h * P, (h + 1) * P)
                        mm = pe.transpose(bank[7][:, s], DD[:, n % 4, s], ident)
                    mm.then_inc(t_done, 1)

                level_y(0)
                for n in range(24):
                    if n + 1 < 24:
                        level_y(n + 1)
                    c = n % 4
                    if n == 20:
                        level_t(19)
                        pe.wait_ge(dt_upd, l * 20 + 20)
                    pe.wait_ge(ym_ready, l * 24 + n + 1)
                    if n < 4:
                        pe.wait_ge(dt_init, l * 4 + c + 1)
                    elif n < 20:
                        pe.wait_ge(dt_upd, l * 20 + n - 3)
                    if 1 <= n < 20:
                        pe.wait_ge(d_upd, l * 20 + n)
                    if n >= 21:
                        pe.wait_ge(dt_fin, l * 4 + n - 20)
                    for h in range(NH):
                        s = slice(h * P, (h + 1) * P)
                        if n < 20:
                            mm = pe.matmul(bank[6][:, s], DTT[:, c, s], YM[:, n % 2, s], start=True, stop=True)
                        else:
                            mm = pe.matmul(bank[7][:, s], YM[:, n % 2, s], DTT[:, c, s], start=True, stop=True)
                    mm.then_inc(p_done, 1)
                    if 1 <= n < 20:
                        level_t(n - 1)

                pe.wait_ge(dt_fin, l * 4 + 4)
                pe.wait_ge(qd_ready, l * 4 + 4)
                for c in range(NC):
                    i = l * NC + c
                    if c >= 1:
                        pe.wait_ge(s_upd, l * 3 + c)
                        for h in range(NH):
                            s = slice(h * P, (h + 1) * P)
                            mm = pe.matmul(bank[4][:, s], KTT[:, h, chunk(c)], ST[:, s], start=True, stop=True)
                        mm.then_inc(ks_done, 1)
                    gemm(l, U_CX + 2 * c)
                    if c >= 1:
                        pe.wait_ge(r_ready, l * 3 + c)
                    for h in range(NH):
                        s = slice(h * P, (h + 1) * P)
                        mm = pe.matmul(bank[5][:, s], DTT[:, c, s], (RR[:, s] if c else VB[:, 0, s]),
                                       start=True, stop=True)
                    mm.then_inc(vn_done, 1)
                    gemm(l, U_CX + 2 * c + 1)
                    pe.wait_ge(vn_ready, i + 1)
                    if c >= 1:
                        pe.wait_ge(o_ready, i)
                    for h in range(NH):
                        s = slice(h * P, (h + 1) * P)
                        mm = pe.matmul(bank[6][:, s], VN[:, s], ATT[:, c, s], start=True, stop=(c == 0))
                        if c >= 1:
                            mm = pe.matmul(bank[6][:, s], ST[:, s], QTT[:, h, chunk(c)], start=False, stop=True)
                    mm.then_inc(o_done, 1)
                    if c < NC - 1:
                        for h in range(NH):
                            s = slice(h * P, (h + 1) * P)
                            mm = pe.matmul(bank[7][:, s], KD[:, c, s], VN[:, s], start=True, stop=True)
                        mm.then_inc(su_done, 1)

                for j in range(4):
                    row_sum(l, 8, j, 4, SQ[j % 2][:, :])
                gemm(l, U_BQK)

                def lru_gates(j):
                    u = U_CX + j
                    pe.wait_ge(bank_free[u % 4], START + l * NBK + u // 4 + 1)
                    if j == 0:
                        pe.wait_ge(rn_rs, l * 3 + 2)
                    elif j == 1:
                        pe.wait_ge(rn_app, l * 16 + 12)
                    else:
                        pe.wait_ge(lru_t, l * 4 + j - 1)
                    b = lru_bank(j)
                    pe.matmul(bank[b][:, :], MP[:, M_WA + j * P:M_WA + (j + 1) * P], XC[:, j, :], start=True, stop=True)
                    pe.matmul(bank[b + 1][:, :], MP[:, M_WX + j * P:M_WX + (j + 1) * P], XC[:, j, :],
                              start=True, stop=True).then_inc(lru_mm, 1)

                lru_gates(0)
                row_broadcast(l, 8, 4, 1)
                for j in range(1, 4):
                    gemm(l, U_BQK + j)
                    lru_gates(j)

                def rotate(i):
                    pe.wait_ge(raw_ready, l * 4 + i + 1)
                    if i < 2:
                        pe.wait_ge(lru_t, l * 4 + 3)
                    else:
                        pe.wait_ge(rot_m2, l * 4 + i - 1)
                    pe.matmul(bank[4 + i % 2][:, :], perm, RAW[:, i, :], start=True, stop=True)\
                      .then_inc(perm_done, 1)

                gemm(l, U_CG)
                rotate(0)
                rotate(1)
                gemm(l, U_CG + 1)
                rotate(2)
                rotate(3)
                gemm(l, U_CG + 2)
                gemm(l, U_CG + 3)

                def turn_v(h):
                    pe.wait_ge(bank_free[(U_BV + h) % 4], START + l * NBK + (U_BV + h) // 4 + 1)
                    if h < 2:
                        pe.wait_ge(rot_m2, l * 4 + h + 3)
                    else:
                        pe.wait_ge(bv_ready, l * 4 + h - 1)
                    for c in range(NC):
                        mm = pe.transpose(bank[4 + h % 2][:, chunk(c)], RAW[:, h, chunk(c)], ident)
                    mm.then_inc(bvt_done, 1)

                def scores(h, j):
                    r = slice(64 * (h % 2), 64 * (h % 2) + 64)
                    n = h * 4 + j
                    if n >= 3:
                        pe.wait_ge(sc_ready, l * 16 + n - 2)
                    pe.matmul(bank[4 + n % 3][:, 0:T - j * P], RQ[r, 2 + h // 2, chunk(j)],
                              RQ[r, h // 2, j * P:T], start=True, stop=True).then_inc(sc_done, 1)

                def values(h):
                    pe.wait_ge(sc_ready, l * 16 + 4 * h + 4)
                    if h >= 1:
                        pe.wait_ge(ob_ready, l * 4 + h)
                    off = 0
                    for j in range(NC):
                        mm = pe.matmul(bank[7][:, j * P:T], BV[:, h, chunk(j)], SC[h % 2][:, off:off + T - j * P],
                                       start=(j == 0), stop=(j == NC - 1), skip_group_check=True)
                        off += T - j * P
                    mm.then_inc(pv_done, 1)

                gemm(l, U_BV)
                gemm(l, U_BV + 1)
                turn_v(0)
                gemm(l, U_BV + 2)
                turn_v(1)
                gemm(l, U_BV + 3)
                turn_v(2)
                gemm(l, U_BG)
                turn_v(3)
                pe.wait_ge(ld_dm, l * 16 + 16)
                pe.wait_ge(rq_ready, l * 4 + 4)
                pe.wait_ge(bv_ready, l * 4 + 4)
                pe.wait_ge(lru_t, l * 4 + 4)
                for j in range(3):
                    scores(0, j)
                gemm(l, U_BG + 1)
                scores(0, 3)
                for j in range(2):
                    scores(1, j)
                gemm(l, U_BG + 2)
                values(0)
                for j in range(2, 4):
                    scores(1, j)
                scores(2, 0)
                gemm(l, U_BG + 3)
                values(1)
                for j in range(1, 4):
                    scores(2, j)
                values(2)
                for j in range(4):
                    scores(3, j)
                gemm(l, U_MIX)
                values(3)
                for h in range(NH):
                    pe.wait_ge(ob_ready, l * 4 + h + 1)
                    if h >= 2:
                        pe.wait_ge(cen_ready, l * 4 + h - 1)
                    pe.matmul(bank[5 + h % 2][:, :], ones, OB[:, h, :], start=True, stop=True).then_inc(mean_done, 1)
                gemm(l, U_MIX + 1)
                for j in range(4):
                    row_sum(l, 12, j, 4, SQ[j % 2][:, :])
                gemm(l, U_MIX + 2)
                row_broadcast(l, 12, 4, 2)

                for d in range(DT_):
                    if d >= 1:
                        for n in range(3):
                            gemm(l, U_MIX + 4 * d + n)
                    u = U_MIX + 4 * d + 3
                    if d == 0:
                        pe.wait_ge(y_lo, l * 12 + 12)
                        pe.wait_ge(rn_app, l * 16 + 16)
                    pe.wait_ge(w_lo, START + l * NU + u + 1)
                    pe.wait_ge(bank_free[3], START + l * NBK + u // 4)
                    if d >= 1:
                        pe.wait_ge(mg_done, l * 8 + d)
                    for n in range(3):
                        product(l, u, bank[3 + n][:, :], 4 * n, y_part, nk=4, last_signal=(n == 2))
                for d in range(DT_):
                    gemm(l, U_OUT + d, arrives=h_arrives(l, 1) if d == 0 else None)
                norm_sums(l, 1)
                for g in range(2):
                    for i in range(2 * PAIRS[g]):
                        gemm(l, U_FFN[g] + i, arrives=h_arrives(l, 2) if g == 0 and i == 0 else None)
                    p0 = 0 if g == 0 else PAIRS[0]
                    for d in range(DT_):
                        gemm(l, U_DOWN[g] + d, y_part,
                             arrives=(lambda k: pe.wait_ge(f_lo, START + l * 22 + p0 + k + 1)) if d == 0 else None)
            norm_sums(L, 0)

        @block.vector
        def _(dve):
            def shift_taps(l, u, dst, width, w0, ready, n_ready, acc, n_acc):
                b = bank[u % 4]
                dve.wait_ge(ready, n_ready)
                for s in range(1, width):
                    if s > 1:
                        dve.wait_ge(acc, n_acc + s - 1)
                    ins = dve.scalar_tensor_tensor(out=dst[:, s:T], in0=b[:, 0:T - s], scalar=w0(width - 1 - s),
                                                   in1=dst[:, s:T], op0=MUL, op1=ADD)
                    ins.then_inc(*((acc, 1) if s < width - 1 else (bank_free[u % 4], 1)))

            def h_rest(l, batch, k, src):
                dve.wait_ge(h_hi, l * 24 + 8 * batch + k + 1)
                dve.tensor_tensor(H[:, k, 1, :], src[:, k, :], H[:, k, 0, :], SUB).then_inc(h_lo[0], 1)

            def norm_apply(l, n, g0, batch):
                dve.wait_ge(rs_done, l * 2 + n + 1)
                dve.reciprocal(ROWI[:, :], ROW[:, :]).then_inc(ri_done, 1)
                dve.wait_ge(ri_done, l * 2 + n + 1)
                for k in range(KT):
                    dve.scalar_tensor_tensor(out=HN[:, k, :], in0=X[:, k, :], scalar=col(MP, g0 + k),
                                             in1=ROWI[:, :], op0=MUL, op1=MUL).then_inc(hn_ready, 1)
                    if k % 2 == 1:
                        h_rest(l, batch, k - 1, HN)

            def rows_inverse(l, n, nth):
                dve.wait_ge(rn_rs, l * 3 + nth + 1)
                dve.reciprocal(ROWI[0:n, :], ROW[0:n, :]).then_inc(rn_ri, 1)

            n_rot = [0]

            def rot(ins):
                ins.then_inc(rot_v, 1)
                n_rot[0] += 1
                dve.wait_ge(rot_v, n_rot[0])

            for b in range(4):
                dve.memset(SM[:, 471 + b:472 + b], 0.0).then_inc(bank_free[b], 1)
            dve.memset(SM[:, 475:476], 0.0).then_inc(f_lo, 1)

            magic = 1.5 * 2.0 ** 23
            turn = (6.28125, 0.0019350051879882812, 3.019916050561733e-07)
            dve.wait_ge(ld_const, 16)
            dve.wait_ge(ld_pos, 16)
            ang, cnt = TM[1][:, :], TM[2][:, :]
            rot(dve.tensor_copy(TM[3][:, :], TM[0][:, :].bitcast(I32)))
            rot(dve.tensor_scalar(ang, TM[3][:, :], CO[:, C_MISC:C_MISC + 1], None, MUL))
            for m in (4096.0, 1.0):
                rot(dve.tensor_scalar(cnt, ang, 1.0 / (2 * 3.141592653589793 * m), magic, MUL, ADD))
                rot(dve.tensor_scalar(cnt, cnt, magic, None, SUB))
                for part in turn:
                    rot(dve.scalar_tensor_tensor(out=ang, in0=cnt, scalar=-part * m, in1=ang, op0=MUL, op1=ADD))
            rot(dve.tensor_scalar(ang, ang, 3.1415925, -3.1415925, MIN, MAX))
            dve.wait_ge(rot_a, 2)
            rot_n = 13
            dve.tensor_tensor(TM[3][:, :], TM[2][:, :], TM[2][:, :], MUL).then_inc(rot_v, 1)
            dve.wait_ge(rot_v, rot_n + 1)
            dve.tensor_scalar(CS[:, 0, :], TM[3][:, :], -2.0, 1.0, MUL, ADD).then_inc(rot_v, 1)
            dve.wait_ge(rot_v, rot_n + 2)
            dve.wait_ge(ld_x, 32)

            with dve.Fori(0, L) as l:
                dve.wait_ge(ld_mp, l * 16 + 16)
                norm_apply(l, 0, M_GA, 0)

                n_s = [0]

                def step(ins):
                    ins.then_inc(sm_v, 1)
                    n_s[0] += 1
                    dve.wait_ge(sm_v, l * 17 + n_s[0])

                ab = bank[5][:, 0:32].rearrange("p (c n) -> p c n", n=8)
                ch = "p (c h) -> p c h"
                dve.wait_ge(ab_done, l + 1)
                dve.wait_ge(sm_a, l * 7 + 1)
                step(dve.tensor_tensor(XS[:, 0:16].rearrange(ch, h=4), ab[:, :, 0:4],
                                       MP[:, M_DT:M_DT + 4].unsqueeze(1).to_broadcast([P, NC, 4]), ADD))
                step(dve.tensor_scalar(XS[:, 16:20], MP[:, M_LAM:M_LAM + 4], -1.0, None, MUL))
                step(dve.scalar_tensor_tensor(out=AX, in0=XS, scalar=-1.0, in1=XS, op0=MUL, op1=MAX))
                dve.wait_ge(sm_a, l * 7 + 4)
                step(dve.tensor_scalar(WM, EX, 1.0, 1.0, ADD, SUB))
                step(dve.tensor_scalar(WM, WM, 1e-30, None, MAX))
                step(dve.reciprocal(RC, WM))
                step(dve.tensor_tensor(RC, RC, EX, MUL))
                step(dve.tensor_tensor(RC, RC, LW, MUL))
                step(dve.scalar_tensor_tensor(out=SP, in0=XS, scalar=0.0, in1=RC, op0=MAX, op1=ADD))
                step(dve.tensor_scalar(SP2, SP[:, 16:20], 2.0, None, MUL))
                step(dve.tensor_scalar(BE, TB, 0.5, 0.5, MUL, ADD))
                step(dve.tensor_scalar(HB, BE, 0.5, None, MUL))
                step(dve.tensor_scalar(HBA, MP[:, M_BA:M_BA + 8], 0.5, None, MUL))
                step(dve.scalar_tensor_tensor(out=GG.rearrange(ch, h=4), in0=SP[:, 0:16].rearrange(ch, h=4),
                                              scalar=-1.0, in1=EA.unsqueeze(1).to_broadcast([P, NC, 4]),
                                              op0=MUL, op1=MUL))

                def silu_conv(u):
                    shift_taps(l, u, TM[u % 2], 4, lambda j: col(MP, M_CW + u * 4 + j), cv_ready, l * 12 + u + 1,
                               cv_acc, l * 24 + 2 * u)
                    dve.wait_ge(th_ready, l * 12 + u + 1)
                    dst = (QTT, KTT, VT)[u // 4][:, u % 4, :]
                    dve.scalar_tensor_tensor(out=dst, in0=TM[2 + u % 2][:, :], scalar=1.0, in1=TM[u % 2][:, :],
                                             op0=ADD, op1=MUL).then_inc(silu_done, 1)

                dve.wait_ge(gc_done, l + 1)
                step(dve.tensor_copy(GCS, bank[5][:, 64:96]))
                step(dve.tensor_tensor(DL, GCS[:, 16:32], GCS[:, 0:16], SUB))
                dve.wait_ge(sm_a, l * 7 + 7)
                step(dve.scalar_tensor_tensor(out=NBG, in0=BE, scalar=-1.0, in1=EGC, op0=MUL, op1=MUL))
                for u in range(11):
                    silu_conv(u)
                rows_inverse(l, 8, 0)
                silu_conv(11)

                def cum_weights(c):
                    if c >= 2:
                        dve.wait_ge(grow_done, l * NC + c - 1)
                    for h in range(NH):
                        ins = dve.tensor_scalar(TM[c % 2][:, h * P:(h + 1) * P], upper, col(GG, c * 4 + h), None, MUL)
                    ins.then_inc(ug_ready, 1)

                dve.wait_ge(silu_done, l * 12 + 12)
                cum_weights(0)
                cum_weights(1)
                for j in range(8):
                    t = QTT[:, j, :] if j < 4 else KTT[:, j - 4, :]
                    dve.wait_ge(rn_b, l * 16 + j + 1)
                    dve.tensor_tensor(t, t, bank[6 + j % 2][:, :], MUL).then_inc(rn_app, 1)

                def prep_1(c):
                    i = l * NC + c
                    if c >= 2:
                        cum_weights(c)
                    dve.wait_ge(grow_done, i + 1)
                    dve.wait_ge(eg_ready, i + 1)
                    for h in range(NH):
                        s = slice(h * P, (h + 1) * P)
                        ins = dve.tensor_scalar(EL[:, c % 2, s], pb(c, 1)[:, s], col(GCS, c * 4 + h), 0.0, SUB, MAX)
                    ins.then_inc(el_pre, 1)

                def prep_2(c):
                    i = l * NC + c
                    dve.wait_ge(el_ready, i + 1)
                    dve.wait_ge(kk_done, i + 1)
                    if c >= 2:
                        dve.wait_ge(tl_done, i - 1)
                        dve.wait_ge(ta_done, i - 1)
                    for h in range(NH):
                        s = slice(h * P, (h + 1) * P)
                        ins = dve.scalar_tensor_tensor(out=TM[4 + c % 2][:, s], in0=pb(c, 2)[:, s],
                                                       scalar=col(BE, c * 4 + h), in1=EL[:, c % 2, s], op0=MUL, op1=MUL)
                    ins.then_inc(l_ready, 1)
                    dve.wait_ge(qk_done, i + 1)
                    dve.tensor_tensor(TM[2 + c % 2][:, :], pb(c, 3), EL[:, c % 2, :], MUL).then_inc(at_ready, 1)
                    dve.wait_ge(l_ready, i + 1)
                    dve.tensor_tensor(heads(DD[:, c, :]), heads(TM[4 + c % 2][:, :]), over_heads(neg_mask(0)), MUL)\
                       .then_inc(d_pre, 1)
                    dve.wait_ge(d_pre, i + 1)
                    dve.tensor_tensor(heads(DD[:, c, :]), heads(DD[:, c, :]), over_heads(ident), ADD)\
                       .then_inc(d_init, 1)

                def prep_3(c):
                    i = l * NC + c
                    dve.wait_ge(ta_done, i + 1)
                    dve.tensor_tensor(heads(ATT[:, c, :]), heads(pb(c, 2)), over_heads(upper), MUL)\
                       .then_inc(att_ready, 1)

                prep_1(0)
                prep_1(1)
                prep_2(0)
                prep_2(1)
                prep_3(0)
                prep_1(2)
                prep_2(2)
                prep_3(1)
                prep_1(3)
                prep_2(3)
                prep_3(2)
                prep_3(3)

                def level_mask(n):
                    i = l * 24 + n
                    dve.wait_ge(y_done, i + 1)
                    if n >= 2:
                        dve.wait_ge(p_done, i - 1)
                    if n == 0:
                        dve.wait_ge(qd_ready, l * 4 + 4)
                    dve.tensor_tensor(heads(YM[:, n % 2, :]), heads(bank[4 + n % 2][:, :]),
                                      over_heads(neg_mask(1 + n // 4)), MUL).then_inc(ym_ready, 1)

                level_mask(0)
                for n in range(24):
                    if n + 1 < 24:
                        level_mask(n + 1)
                    c = n % 4
                    dve.wait_ge(p_done, l * 24 + n + 1)
                    if n < 20:
                        dve.tensor_tensor(DD[:, c, :], DD[:, c, :], bank[6][:, :], ADD).then_inc(d_upd, 1)
                    else:
                        dve.tensor_tensor(DTT[:, c, :], DTT[:, c, :], bank[7][:, :], ADD).then_inc(dt_fin, 1)

                def gate_silu(u, nth, dst, done_sem):
                    dve.wait_ge(zt_ready, l * 8 + nth + 1)
                    dve.scalar_tensor_tensor(out=dst, in0=TM[2 + u % 2][:, :], scalar=1.0, in1=bank[u % 4][:, :],
                                             op0=ADD, op1=MUL).then_inc(bank_free[u % 4], 1)

                def fill(n):
                    u = U_CX + n
                    if n < 4:
                        shift_taps(l, u, XC[:, n, :], 4, lambda j: col(MP, M_LW + n * 4 + j), xc_ready, l * 4 + n + 1,
                                   lru_acc, l * 8 + 2 * n)
                    else:
                        gate_silu(u, n - 4, ZS[:, n - 4, :], None)

                for c in range(NC):
                    if c >= 1:
                        dve.wait_ge(ks_done, l * 3 + c)
                        dve.wait_ge(vn_done, l * 4 + c)
                        for h in range(NH):
                            s = slice(h * P, (h + 1) * P)
                            ins = dve.scalar_tensor_tensor(out=RR[:, s], in0=bank[4][:, s], scalar=col(NBG, c * 4 + h),
                                                           in1=VB[:, c, s], op0=MUL, op1=ADD)
                        ins.then_inc(r_ready, 1)
                    fill(2 * c)
                    fill(2 * c + 1)
                    if c < NC - 1:
                        dve.wait_ge(su_done, l * 3 + c + 1)
                        if c == 0:
                            dve.tensor_copy(ST[:, :], bank[7][:, :]).then_inc(s_upd, 1)
                        else:
                            dve.wait_ge(s_upd, l * 3 + c)
                            for h in range(NH):
                                s = slice(h * P, (h + 1) * P)
                                ins = dve.scalar_tensor_tensor(out=ST[:, s], in0=ST[:, s], scalar=col(EGT, c * 4 + h),
                                                               in1=bank[7][:, s], op0=MUL, op1=ADD)
                            ins.then_inc(s_upd, 1)

                rows_inverse(l, 4, 1)
                for j in range(4):
                    dve.wait_ge(rn_b, l * 16 + 8 + j + 1)
                    dve.scalar_tensor_tensor(out=OT[:, j, :], in0=OT[:, j, :], scalar=col(MP, M_NW),
                                             in1=bank[6 + j % 2][:, :], op0=MUL, op1=MUL).then_inc(rn_app, 1)
                    dve.wait_ge(rn_app, l * 16 + 8 + j + 1)
                    dve.scalar_tensor_tensor(out=OT[:, j, :], in0=ZS[:, j, :], scalar=0.5, in1=OT[:, j, :],
                                             op0=MUL, op1=MUL).then_inc(y_fin, 1)

                def y_rest(nth, t, src):
                    dve.wait_ge(y_hi, l * 12 + nth + 1)
                    dve.tensor_tensor(Y[:, t, 1, :], src, Y[:, t, 0, :], SUB).then_inc(y_lo, 1)

                for i in range(4):
                    u = U_BQK + i
                    dve.wait_ge(raw_ready, l * 4 + i + 1)
                    dve.tensor_tensor(RQ[:, i, :], bank[u % 4][:, :], CS[:, 0, :], MUL).then_inc(bank_free[u % 4], 1)
                for j in range(4):
                    dve.wait_ge(lru_th, l * 4 + j + 1)
                    dve.tensor_scalar(INV[:, j, :], TH[:, j, :], 1.0, None, ADD).then_inc(lru_v, 1)
                for i in range(4):
                    u = U_BQK + i
                    dve.wait_ge(perm_done, l * 4 + i + 1)
                    if i >= 2:
                        dve.wait_ge(rq_ready, l * 4 + i - 1)
                    dve.tensor_tensor(TM[i % 2][:, :], bank[4 + i % 2][:, :], CS[:, 1, :], MUL).then_inc(rot_m2, 1)
                    dve.wait_ge(rot_m2, l * 4 + i + 1)
                    dve.wait_ge(bank_free[u % 4], START + l * NBK + u // 4 + 1)
                    dve.tensor_tensor(RQ[:, i, :], RQ[:, i, :], TM[i % 2][:, :], ADD).then_inc(rq_ready, 1)
                for i in range(4):
                    y_rest(i, i, OT[:, i, :])

                def lru(j):
                    v0 = l * 28 + 4 + j * 6
                    dve.wait_ge(lru_v, v0)
                    dve.reciprocal(INV[:, j, :], INV[:, j, :]).then_inc(lru_v, 1)
                    dve.scalar_tensor_tensor(out=TI[:, j, :], in0=TI[:, j, :], scalar=1.0, in1=XC[:, j, :],
                                             op0=ADD, op1=MUL).then_inc(lru_v, 1)
                    dve.wait_ge(lru_v, v0 + 2)
                    dve.tensor_tensor(TI[:, j, :], TI[:, j, :], INV[:, j, :], MUL).then_inc(lru_v, 1)
                    dve.wait_ge(lru_v, v0 + 3)
                    dve.tensor_scalar(INV[:, j, :], INV[:, j, :], 2.0, -1.0, MUL, ADD).then_inc(lru_v, 1)
                    dve.wait_ge(lru_sq, l * 4 + j + 1)
                    dve.tensor_tensor(TI[:, j, :], TI[:, j, :], TH[:, j, :], MUL).then_inc(lru_v, 1)
                    dve.wait_ge(lru_v, v0 + 5)
                    dve.tensor_tensor_scan(XC[:, j, :], INV[:, j, :], TI[:, j, :], 0.0, MUL, ADD).then_inc(lru_v, 1)

                def gelu_1(j):
                    t, b = TM[j % 2][:, :], bank[(U_CG + j) % 4][:, :]
                    dve.wait_ge(ge_a, l * 4 + j + 1)
                    dve.tensor_scalar(t, t, 0.044715, 1.0, MUL, ADD).then_inc(ge_v, 1)
                    dve.wait_ge(ge_v, l * 8 + 2 * j + 1)
                    dve.tensor_tensor(t, t, b, MUL).then_inc(ge_v, 1)

                def gelu_2(j):
                    u = U_CG + j
                    t, yt = TM[j % 2][:, :], TM[4 + j % 2][:, :]
                    dve.wait_ge(ge_t, l * 4 + j + 1)
                    dve.scalar_tensor_tensor(out=t, in0=t, scalar=1.0, in1=bank[u % 4][:, :],
                                             op0=ADD, op1=MUL).then_inc(bank_free[u % 4], 1)
                    dve.wait_ge(bank_free[u % 4], START + l * NBK + u // 4 + 1)
                    dve.wait_ge(lru_v, l * 28 + 10 + j * 6)
                    if j >= 2:
                        dve.wait_ge(y_lo, l * 12 + 4 + j - 1)
                    dve.scalar_tensor_tensor(out=yt, in0=t, scalar=0.5, in1=XC[:, j, :],
                                             op0=MUL, op1=MUL).then_inc(y_fin, 1)

                lru(0)
                gelu_1(0)
                for j in range(1, 4):
                    lru(j)
                    gelu_2(j - 1)
                    gelu_1(j)
                    y_rest(4 + j - 1, 8 + j - 1, TM[4 + (j - 1) % 2][:, :])
                gelu_2(3)
                y_rest(7, 11, TM[5][:, :])

                def scores(h, j):
                    n = h * 4 + j
                    off = sum(T - i * P for i in range(j))
                    dve.wait_ge(sc_done, l * 16 + n + 1)
                    if h >= 2 and j == 0:
                        dve.wait_ge(pv_done, l * 4 + h - 1)
                    dve.tensor_tensor(SC[h % 2][:, off:off + T - j * P], bank[4 + n % 3][:, 0:T - j * P],
                                      CO[:, C_DM + h * T:C_DM + (h + 1) * T - j * P], MUL).then_inc(sc_ready, 1)

                def bg(h):
                    u = U_BG + h
                    dve.wait_ge(bvt_done, l * 4 + 4)
                    gate_silu(u, 4 + h, BGS[:, h, :], None)

                bg(0)
                for j in range(4):
                    scores(0, j)
                bg(1)
                for j in range(3):
                    scores(1, j)
                bg(2)
                scores(1, 3)
                for j in range(2):
                    scores(2, j)
                bg(3)
                dve.memset(SM[:, 476:477], 0.0).then_inc(bg_ready, 4)
                for j in range(2, 4):
                    scores(2, j)
                for j in range(4):
                    scores(3, j)
                for h in range(NH):
                    dve.wait_ge(mean_done, l * 4 + h + 1)
                    dve.scalar_tensor_tensor(out=OB[:, h, :], in0=bank[5 + h % 2][:, :], scalar=-1.0 / P,
                                             in1=OB[:, h, :], op0=MUL, op1=ADD).then_inc(cen_ready, 1)
                rows_inverse(l, 4, 2)
                dve.wait_ge(bank_free[(U_BG + 3) % 4], START + l * NBK + (U_BG + 3) // 4 + 1)
                for j in range(4):
                    dve.wait_ge(rn_b, l * 16 + 12 + j + 1)
                    dve.tensor_tensor(OB[:, j, :], OB[:, j, :], bank[6 + j % 2][:, :], MUL).then_inc(rn_app, 1)
                    dve.wait_ge(rn_app, l * 16 + 12 + j + 1)
                    dve.scalar_tensor_tensor(out=OB[:, j, :], in0=BGS[:, j, :], scalar=0.5, in1=OB[:, j, :],
                                             op0=MUL, op1=MUL).then_inc(y_fin, 1)
                for h in range(4):
                    y_rest(8 + h, 4 + h, OB[:, h, :])

                for d in range(DT_):
                    dve.wait_ge(gemm_done, START + l * NU + U_MIX + 4 * d + 4)
                    for n in range(3):
                        dve.wait_ge(bank_free[n], START + l * NBK + (U_MIX + 4 * d) // 4 + 1)
                    dve.scalar_tensor_tensor(out=MM[:, d, :], in0=GT[:, d % 2, 0, :], scalar=1.0, in1=bank[3][:, :],
                                             op0=ADD, op1=MUL).then_inc(bank_free[3], 1)
                    dve.scalar_tensor_tensor(out=TM[0][:, :], in0=GT[:, d % 2, 1, :], scalar=1.0, in1=bank[4][:, :],
                                             op0=ADD, op1=MUL).then_inc(mg_v, 1)
                    if d >= 1:
                        dve.wait_ge(hn_ready, l * 24 + 8 + d)
                    dve.scalar_tensor_tensor(out=TM[1][:, :], in0=GT[:, d % 2, 2, :], scalar=1.0, in1=bank[5][:, :],
                                             op0=ADD, op1=MUL).then_inc(mg_done, 1)
                    dve.wait_ge(mg_v, l * 16 + 2 * d + 1)
                    dve.wait_ge(bank_free[3], START + l * NBK + (U_MIX + 4 * d) // 4 + 1)
                    dve.tensor_tensor(MM[:, d, :], MM[:, d, :], TM[0][:, :], ADD).then_inc(mg_v, 1)
                    dve.wait_ge(mg_v, l * 16 + 2 * d + 2)
                    dve.wait_ge(mg_done, l * 8 + d + 1)
                    dve.tensor_tensor(MM[:, d, :], MM[:, d, :], TM[1][:, :], ADD).then_inc(hn_ready, 1)
                for k in range(0, KT, 2):
                    h_rest(l, 1, k, MM)
                for d in range(DT_):
                    u = U_OUT + d
                    dve.wait_ge(gemm_done, START + l * NU + u + 1)
                    dve.scalar_tensor_tensor(out=X[:, d, :], in0=bank[u % 4][:, :], scalar=0.5, in1=X[:, d, :],
                                             op0=MUL, op1=ADD).then_inc(bank_free[u % 4], 1)
                for b in range(4):
                    dve.wait_ge(bank_free[b], START + l * NBK + (U_OUT + 7) // 4 + 1)
                norm_apply(l, 1, M_GF, 2)

                dve.wait_ge(ld_fp, l * 16 + 16)
                p0 = 0
                for g in range(2):
                    for i in range(PAIRS[g]):
                        p, u = p0 + i, U_FFN[g] + 2 * i
                        shift_taps(l, u, CG[:, p % 2, :], 3, lambda j: col(FP, F_W + p * 3 + j), fc_ready,
                                   l * 44 + 2 * p + 1, fc_acc, l * 44 + 2 * p)
                        dve.wait_ge(ft_ready, l * 22 + p + 1)
                        dve.scalar_tensor_tensor(out=CG[:, p % 2, :], in0=TG[:, p % 2, :], scalar=1.0,
                                                 in1=CG[:, p % 2, :], op0=ADD, op1=MUL).then_inc(fg_v, 1)
                        shift_taps(l, u + 1, CV[:, p % 2, :], 3, lambda j: col(FP, F_W + (22 + p) * 3 + j), fc_ready,
                                   l * 44 + 2 * p + 2, fc_acc, l * 44 + 2 * p + 1)
                        dve.wait_ge(fg_v, l * 22 + p + 1)
                        dve.wait_ge(bank_free[(u + 1) % 4], START + l * NBK + (u + 1) // 4 + 1)
                        dve.scalar_tensor_tensor(out=CV[:, p % 2, :], in0=CG[:, p % 2, :], scalar=0.5,
                                                 in1=CV[:, p % 2, :], op0=MUL, op1=MUL).then_inc(fg_done, 1)
                        dve.wait_ge(f_hi, l * 22 + p + 1)
                        dve.tensor_tensor(Y[:, i, 1, :], CV[:, p % 2, :], Y[:, i, 0, :], SUB).then_inc(f_lo, 1)
                    for d in range(DT_):
                        u = U_DOWN[g] + d
                        dve.wait_ge(gemm_done, START + l * NU + u + 1)
                        dve.tensor_tensor(X[:, d, :], X[:, d, :], bank[u % 4][:, :], ADD).then_inc(bank_free[u % 4], 1)
                    p0 += PAIRS[g]
                for b in range(4):
                    dve.wait_ge(bank_free[b], START + l * NBK + NBK)

            dve.wait_ge(rs_done, L * 2 + 1)
            dve.reciprocal(ROWI[:, :], ROW[:, :]).then_inc(ri_done, 1)
            dve.wait_ge(ri_done, L * 2 + 1)
            for k in range(KT):
                dve.scalar_tensor_tensor(out=HN[:, k, :], in0=X[:, k, :], scalar=col(FN, k), in1=ROWI[:, :],
                                         op0=MUL, op1=MUL).then_inc(out_ready, 1)


def shape_constants():
    import numpy as np
    i = np.arange(P)
    c = np.zeros((P, NCONST), np.float32)
    c[:, C_ID:C_ID + P] = np.eye(P)
    c[:, C_ONE:C_ONE + P] = 1
    c[:, C_U:C_U + P] = i[:, None] <= i[None, :]
    for h in range(2):
        for m in range(32):
            c[64 * h + m + 32, C_PERM + 64 * h + m] = -1
            c[64 * h + m, C_PERM + 64 * h + m + 32] = 1
    for lv in range(7):
        s = 1 << lv
        m = (i[:, None] // (2 * s) == i[None, :] // (2 * s)) & (i[:, None] // s > i[None, :] // s)
        c[:, C_NEG + lv * P:C_NEG + (lv + 1) * P] = -m.astype(np.float32)
        if lv == 0:
            c[:, C_M1T:C_M1T + P] = -m.T.astype(np.float32)
    lg = np.log(np.float32(1.0) - np.float32(2.0) ** (-5.0 - np.arange(NH, dtype=np.float32))).astype(np.float64)
    x = np.arange(T)
    for h in range(NH):
        d = x[None, :] - i[:, None]
        c[:, C_DM + h * T:C_DM + (h + 1) * T] = np.where(d >= 0, np.exp(np.maximum(d, 0) * lg[h]) * 64 ** -0.5, 0)
    c[:, C_Z15 + 7] = 1
    c[:, C_MISC] = (np.float32(10000.0) ** (-(i % 32).astype(np.float32) / np.float32(32))).astype(np.float32)
    c[0:4, C_MISC + 1], c[4:8, C_MISC + 1] = 128, 1
    c[0:4, C_MISC + 2], c[4:8, C_MISC + 2] = 128 * 4 * EPS, 4 * EPS
    c[:, C_MISC + 3] = EPS
    return c


def kernel(**inp):
    import numpy as np
    from concourse import bacc
    from concourse.bass_utils import run_bass_kernel_spmd as run

    a = {k: np.asarray(v) for k, v in inp.items()}

    def cols(v, n):
        return v.reshape(n, P).T

    def w_units(w):
        k, n = w.shape[0] // P, w.shape[1] // P
        return w.reshape(k, P, n, P).transpose(2, 1, 0, 3).reshape(n, P, k * P)

    wst = np.zeros((L * NU, P, SLOT), np.float32)
    mp = np.zeros((L, P, NMP), np.float32)
    fp = np.zeros((L, P, NFP), np.float32)
    for l in range(L):
        def put(u, units):
            wst[l * NU + u:l * NU + u + len(units), :, :units.shape[2]] = units
        w = a["w_in"][l]
        o = {"qkv": 0, "ab": 1536, "z": 1544, "bq": 2056, "bk": 2312, "bv": 2568, "bg": 3080, "cx": 3592, "cg": 4104,
             "gate": 4616}
        put(U_QKV, w_units(w[:, 0:1536]))
        put(U_Z, w_units(w[:, o["z"]:o["z"] + 512]))
        put(U_BG, w_units(w[:, o["bg"]:o["bg"] + 512]))
        put(U_BQK, w_units(w[:, o["bq"]:o["bq"] + 512]))
        put(U_BV, w_units(w[:, o["bv"]:o["bv"] + 512]))
        put(U_CX, w_units(w[:, o["cx"]:o["cx"] + 512]))
        put(U_CG, w_units(w[:, o["cg"]:o["cg"] + 512]))
        gates = w_units(w[:, o["gate"]:])
        br = w_units(a["w_branch"][l].reshape(12 * P, D))
        for d in range(DT_):
            for n in range(3):
                put(U_MIX + 4 * d + n, gates[8 * n + d][None])
            put(U_MIX + 4 * d + 3, br[d][None])
        put(U_OUT, w_units(a["w_out"][l]))
        up, down = w_units(a["w_up"][l]), a["w_down"][l]
        p0 = 0
        for g in range(2):
            for i in range(PAIRS[g]):
                put(U_FFN[g] + 2 * i, up[p0 + i][None])
                put(U_FFN[g] + 2 * i + 1, up[22 + p0 + i][None])
            put(U_DOWN[g], w_units(down[p0 * P:(p0 + PAIRS[g]) * P]))
            p0 += PAIRS[g]
        m = mp[l]
        m[:, M_GA:M_GA + 8] = cols(a["attn_norm"][l], 8)
        m[:, M_GF:M_GF + 8] = cols(a["ffn_norm"][l], 8)
        m[:, M_CW:M_CW + 48] = a["dn_conv_w"][l].reshape(4, 12, P).transpose(2, 1, 0).reshape(P, 48)
        m[:, M_NW] = a["dn_norm_w"][l]
        m[:, M_LW:M_LW + 16] = a["lru_conv_w"][l].reshape(4, 4, P).transpose(2, 1, 0).reshape(P, 16)
        m[:, M_LB:M_LB + 4] = cols(a["lru_conv_b"][l], 4)
        m[:, M_BA:M_BA + 4] = a["lru_ba"][l].T
        m[:, M_BX:M_BX + 4] = a["lru_bx"][l].T
        m[:, M_LAM:M_LAM + 4] = cols(a["lru_lambda"][l], 4)
        m[:, M_DT:M_DT + 4] = a["dn_dt_bias"][l][None]
        m[:, M_ALOG:M_ALOG + 4] = a["dn_a_log"][l][None]
        m[:, M_WAB:M_WAB + 64] = w[:, 1536:1544].reshape(8, P, 8).transpose(1, 0, 2).reshape(P, 64)
        m[:, M_WA:M_WA + 512] = a["lru_wa"][l].transpose(1, 0, 2).reshape(P, 512)
        m[:, M_WX:M_WX + 512] = a["lru_wx"][l].transpose(1, 0, 2).reshape(P, 512)
        fp[l, :, F_W:F_W + 132] = a["ffn_conv_w"][l].reshape(3, 44, P).transpose(2, 1, 0).reshape(P, 132)
        fp[l, :, F_B:F_B + 44] = cols(a["ffn_conv_b"][l], 44)
    arrays = {
        "consts": shape_constants(),
        "pos": np.ascontiguousarray(np.broadcast_to(a["positions"], (P, T))),
        "x": np.ascontiguousarray(a["x"][0].T.reshape(KT, P, T).transpose(1, 0, 2)),
        "wst": wst, "mp": mp, "fp": fp, "fn": np.ascontiguousarray(cols(a["final_norm"], 8)),
    }
    nc = bacc.Bacc("TRN2", target_bir_lowering=False, num_devices=1, dynamic_dma_scratch_size=1024)
    aps = [nc.dram_tensor(n, list(v.shape), mybir.dt.from_np(v.dtype), kind="ExternalInput").ap()
           for n, v in arrays.items()]
    o = nc.dram_tensor("out", [P, KT, T], F32, kind="ExternalOutput").ap()
    nc.disable_value_cache = True
    build(nc, *aps, o)
    r = np.asarray(run(nc, [arrays], core_ids=[0]).results[0]["out"])
    return np.ascontiguousarray(r.transpose(1, 0, 2).reshape(D, T).T)[None]
```

```python
from contextlib import ExitStack

import concourse.bass as bass
from concourse import mybir

F32 = mybir.dt.float32
F32R = mybir.dt.float32r
I32 = mybir.dt.int32
ACT = mybir.ActivationFunctionType
ALU = mybir.AluOpType
MUL, ADD, SUB, MAX, MIN = ALU.mult, ALU.add, ALU.subtract, ALU.max, ALU.min

P = 128
T = 512
D = 1024
KT = D // P
L = 2
NC = T // P
NH = 4
EPS = 1e-6
NLV = 6
DT_ = 8

U_QKV, U_CX, U_Z, U_BQK, U_CG, U_BV, U_BG = 0, 12, 16, 20, 24, 28, 32
U_MIX = 36
U_OUT = U_MIX + 4 * DT_
U_FFN = (U_OUT + DT_, U_OUT + DT_ + 24 + DT_)
PAIRS = (12, 10)
U_DOWN = (U_FFN[0] + 24, U_FFN[1] + 20)
NU = U_DOWN[1] + DT_
SLOT = 12 * P
NST = 4
NBK = NU // 4
START = 1

C_ID, C_ONE, C_U, C_PERM, C_M1T = 0, P, 2 * P, 3 * P, 4 * P
C_NEG = 5 * P
C_MISC = C_NEG + 7 * P
C_DM = C_MISC + 4
NCONST = C_DM + NH * T
M_GA, M_GF, M_CW, M_NW, M_LW, M_LB, M_BA, M_BX = 0, 8, 16, 64, 65, 81, 85, 89
M_LAM, M_DT, M_ALOG, M_WAB = 93, 97, 101, 105
M_WA = M_WAB + 64
M_WX = M_WA + 512
NMP = M_WX + 512 + 7
F_W, F_B = 0, 132
NFP = 176


def unit_k(u):
    if u >= U_MIX and u < U_OUT:
        return 12 if (u - U_MIX) % 4 == 3 else 8
    if U_DOWN[0] <= u < U_DOWN[0] + 8:
        return 12
    if u >= U_DOWN[1]:
        return 10
    return 8


def build(nc, consts, posd, x_in, wst, mpd, fpd, fnd, out):
    with ExitStack() as ctx:
        base = -(-nc.sbuf_base // 64) * 64
        place = {"at": base}

        def sb(name, shape, dt=F32, at=None):
            n = 4
            for s in shape[1:]:
                n *= s
            off = place["at"] if at is None else at
            if at is None:
                place["at"] += -(-n // 32) * 32
            return nc.alloc_sbuf_tensor_at(name, shape, dt, offset=off)

        X = sb("x_res", [P, KT, T])
        H = sb("h_parts", [P, KT, 2, T], F32R)
        STG = sb("w_stage", [P, NST, SLOT])
        SPL = sb("w_parts", [P, 2, 2, SLOT], F32R)
        y_at = place["at"]
        Y = sb("y_parts", [P, 12, 2, T], F32R)
        CO = sb("consts", [P, NCONST])
        CS = sb("cos_sin", [P, 2, T])
        MP = sb("mixer_params", [P, NMP])
        WAB = sb("ab_parts", [P, 2, 8, 8], F32R)
        SM = sb("small", [P, 412])
        FP = MP[:, M_WA:M_WA + NFP]
        FN = SM[:, 404:412]
        left_at = place["at"]
        KK = [sb(f"area{i}", [P, 4, T]) for i in range(5)]
        TM = [sb(f"tmp{i}", [P, T]) for i in range(6)]

        VT = sb("dn_vT", [P, 4, T], at=y_at)
        ST = [sb(f"dn_state{i}", [P, T], at=y_at + 6144 * i) for i in range(2)]
        RR = sb("dn_r", [P, T], at=y_at + 2048)
        VN = sb("dn_vnew", [P, T], at=y_at + 4096)
        EG = sb("dn_eg", [P, 2, T], at=y_at + 8192)
        YM = sb("dn_ym", [P, 2, T], at=y_at + 8192)
        EL = sb("dn_el", [P, 2, T], at=y_at + 12288)
        DTT = sb("dn_tT", [P, NC, T], at=y_at + 16384)
        OT = sb("dn_out", [P, 4, T], at=y_at + 24576)
        DD = sb("dn_t", [P, NC, T], at=y_at + 32768)
        LT = sb("dn_lT", [P, NC, T], at=y_at + 40960)
        ZS = sb("z_silu", [P, 4, T], at=y_at + 32768)
        BGS = sb("bg_silu", [P, 4, T], at=y_at + 24576)
        RAW = sb("ret_raw", [P, 4, T], at=y_at + 16384)
        XC = [sb("lru_x0", [P, T])] + [sb(f"lru_x{i}", [P, T], at=y_at + 40960 + 2048 * i) for i in range(1, 4)]
        KTT, QTT, ATT, VB, KD = KK
        RQ, BV, OB = KK[0], KK[1], KK[4]
        SC = [sb(f"ret_sc{i}", [P, 1280], at=left_at + 16384 + 5120 * i) for i in range(2)]
        TI, TH, INV = KK[2], KK[3], KK[4]
        MM = sb("merged", [P, 8, T], at=left_at)
        GT = sb("gates", [P, 2, 4, T], at=left_at + 16384)
        assert place["at"] <= nc.sbuf_usable_end, (place["at"], nc.sbuf_usable_end)
        SQN = KK[4]
        HN = sb("normed", [P, KT, T], at=left_at)
        CG, TG, CV, SQ = KK[0], KK[1], KK[2], [TM[2], TM[3]]

        bank = [ctx.enter_context(nc.psum_tensor(f"bank{i}", [P, T], F32)) for i in range(8)]

        def sem(name):
            return ctx.enter_context(nc.semaphore(name))

        ld_const, ld_pos, ld_mp, ld_fp = (sem(n) for n in ("ld_const", "ld_pos", "ld_mp", "ld_fp"))
        ld_x = [sem(f"ld_x{i}") for i in range(2)]
        ld_w = [sem(f"ld_w{i}") for i in range(NST)]
        w_hi, w_lo, gemm_done = sem("w_hi"), sem("w_lo"), sem("gemm_done")
        bank_free = [sem(f"bank_free{i}") for i in range(4)]
        rot_v, rot_a = sem("rot_v"), sem("rot_a")
        sq_sum, nt_done, nt_row, nb_done = (sem(n) for n in ("sq_sum", "nt_done", "nt_row", "nb_done"))
        rn_tp, rn_tr = sem("rn_tp"), sem("rn_tr")
        sq_ready, norm_mm, rs_done, ri_done = sem("sq_ready"), sem("norm_mm"), sem("rs_done"), sem("ri_done")
        hn_ready, h_hi = sem("hn_ready"), sem("h_hi")
        h_lo = (sem("h_lo_even"), sem("h_lo_odd"))
        wab_hi, wab_lo, ab_mm, ab_row, ab_done = (sem(n) for n in ("wab_hi", "wab_lo", "ab_mm", "ab_row", "ab_done"))
        sm_v, sm_a, gc_done = sem("sm_v"), sem("sm_a"), sem("gc_done")
        cv_ready, cv_acc, th_ready, silu_done = sem("cv_ready"), sem("cv_acc"), sem("th_ready"), sem("silu_done")
        rn_sq, rn_mm, rn_rs, rn_ri, rn_b, rn_app = (sem("rn_" + n) for n in ("sq", "mm", "rs", "ri", "b", "app"))
        ug_ready, grow_done, eg_ready, el_pre, el_ready = (
            sem(n) for n in ("ug_ready", "grow_done", "eg_ready", "el_pre", "el_ready"))
        kk_done, qk_done, l_ready, at_ready, qd_ready = (
            sem(n) for n in ("kk_done", "qk_done", "l_ready", "at_ready", "qd_ready"))
        tv_done, tk_done, tl_done, ta_done = (sem(n) for n in ("tv_done", "tk_done", "tl_done", "ta_done"))
        vb_ready, kd_ready, lt_ready, att_ready = (sem(n) for n in ("vb_ready", "kd_ready", "lt_ready", "att_ready"))
        d_pre, d_init, dt_pre, dt_init = (sem(n) for n in ("d_pre", "d_init", "dt_pre", "dt_init"))
        y_done, ym_ready, p_done, t_done, d_upd, dt_upd, dt_fin = (
            sem(n) for n in ("y_done", "ym_ready", "p_done", "t_done", "d_upd", "dt_upd", "dt_fin"))
        ks_done, r_ready, vn_done, vn_ready, o_done, o_ready, su_done, s_upd = (
            sem(n) for n in ("ks_done", "r_ready", "vn_done", "vn_ready", "o_done", "o_ready", "su_done", "s_upd"))
        zt_ready, y_fin, y_hi, y_lo = sem("zt_ready"), sem("y_fin"), sem("y_hi"), sem("y_lo")
        raw_ready, perm_done, rot_m2, rq_ready = (
            sem(n) for n in ("raw_ready", "perm_done", "rot_m2", "rq_ready"))
        bvt_done, bv_ready, sc_done, sc_ready, pv_done, ob_ready = (
            sem(n) for n in ("bvt_done", "bv_ready", "sc_done", "sc_ready", "pv_done", "ob_ready"))
        mean_done, cen_ready = sem("mean_done"), sem("cen_ready")
        xc_ready, lru_acc, lru_mm, lru_t, lru_th, lru_sq, lru_v = (
            sem(n) for n in ("xc_ready", "lru_acc", "lru_mm", "lru_t", "lru_th", "lru_sq", "lru_v"))
        ge_a, ge_t, ge_v, mg_v, mg_done = (sem(n) for n in ("ge_a", "ge_t", "ge_v", "mg_v", "mg_done"))
        fc_ready, fc_acc, ft_ready, fg_v, fg_done, f_hi, f_lo = (
            sem(n) for n in ("fc_ready", "fc_acc", "ft_ready", "fg_v", "fg_done", "f_hi", "f_lo"))
        out_ready, stored, ld_dm = sem("out_ready"), sem("stored"), sem("ld_dm")

        block = ctx.enter_context(nc.Block())

        ident, ones, upper, perm = (CO[:, c:c + P] for c in (C_ID, C_ONE, C_U, C_PERM))
        neg_m1t = CO[:, C_M1T:C_M1T + P]
        eps_col = CO[:, C_MISC + 3:C_MISC + 4]

        def neg_mask(lv):
            return CO[:, C_NEG + lv * P:C_NEG + (lv + 1) * P]

        def over_heads(m):
            return m.unsqueeze(1).to_broadcast([P, NH, P])

        def heads(t):
            return t.rearrange("p (h n) -> p h n", h=NH)

        def col(t, i):
            return t[:, i:i + 1]

        def chunk(c):
            return slice(c * P, (c + 1) * P)

        def pb(c, role):
            return bank[(4 if c % 2 == 0 else 0) + role][:, :]

        def qk_sq(j):
            return (EL, EG)[j // 2 % 2][:, j % 2, :]

        def score_bank(n):
            return bank[4 + (n + 2) % 3]

        def row_bank(b0, j):
            return bank[4 + j % 4 if b0 == 0 else 6 + j % 2][:, :]

        def sq_slot(k):
            return 0 if k == 0 else 1 + (k - 1) % 3

        def lru_bank(j):
            return 4 + (j % 2) * 2

        n_sm = [0]

        def small(n):
            n_sm[0] += n
            assert n_sm[0] <= 396
            return SM[:, n_sm[0] - n:n_sm[0]]

        XS, AX, EX, WM, RC, LW, SP = (small(20) for _ in range(7))
        TB, BE, HB, GG, GCS, DL, EGC, EGT, EKD, NBG = (
            small(16), small(16), small(16), small(16), small(32), small(16), small(16), small(16), small(16), small(16))
        EA, SP2, HBA = small(4), small(4), small(8)
        NR, NI = small(32), small(32)
        ROW, ROWI = TM[4], TM[5]

        @block.sync
        def _(sp):
            sp.dma_start(CO[:, C_MISC:C_DM], consts[:, C_MISC:C_DM]).then_inc(ld_pos, 16)
            sp.dma_start(TM[0][:, :].bitcast(I32), posd).then_inc(ld_pos, 16)
            for half in range(2):
                tiles = slice(half * KT // 2, (half + 1) * KT // 2)
                sp.dma_start(X[:, tiles, :], x_in[:, tiles, :]).then_inc(ld_x[half], 16)
            sp.dma_start(CO[:, 0:C_MISC], consts[:, 0:C_MISC]).then_inc(ld_const, 16)
            sp.dma_start(FN, fnd).then_inc(ld_const, 16)
            with sp.Fori(0, L) as l:
                sp.wait_ge(f_lo, START + l * 22)
                sp.dma_start(MP[:, :], mpd[bass.ds(l, 1), :, :].rearrange("l p n -> (l p) n")).then_inc(ld_mp, 16)
                for u in range(NU):
                    sp.wait_ge(w_lo, START + l * NU + max(u - 3, 0))
                    n = unit_k(u) * P
                    sp.dma_start(STG[:, u % NST, 0:n],
                                 wst[bass.ds(l * NU + u, 1), :, 0:n].rearrange("l p n -> (l p) n"))\
                      .then_inc(ld_w[u % NST], 16)
                    if u == 12:
                        sp.dma_start(CO[:, C_DM:NCONST], consts[:, C_DM:NCONST]).then_inc(ld_dm, 16)
                    if u == 40:
                        sp.dma_start(FP, fpd[bass.ds(l, 1), :, :].rearrange("l p n -> (l p) n"))\
                          .then_inc(ld_fp, 16)
            for k in range(KT):
                sp.wait_ge(out_ready, k + 1)
                sp.dma_start(out[:, k, :], HN[:, k, :]).then_inc(stored, 16)
            sp.wait_ge(stored, 16 * KT)

        @block.scalar
        def _(act):
            def split_hi(l, u):
                act.wait_ge(ld_w[u % NST], 16 * (l * NBK) + 16 * (u // 4 + 1))
                act.wait_ge(gemm_done, START + l * NU + max(u - 1, 0))
                n = unit_k(u) * P
                act.activation(SPL[:, u % 2, 0, 0:n], STG[:, u % NST, 0:n], ACT.Copy).then_inc(w_hi, 1)

            def next_split(l, u):
                if u + 2 < NU:
                    split_hi(l, u + 2)

            def done(l, u):
                act.wait_ge(gemm_done, START + l * NU + u + 1)

            def load_sqrt():
                act.activation(SM[:, 403:404], eps_col, ACT.Sqrt)

            def norm_square(l, n, k):
                if k >= 4:
                    act.wait_ge(sq_sum, l * 12 + n * 6 + k - 3)
                elif k == 0:
                    act.wait_ge(norm_mm, START + l * 2 + n)
                act.activation(SQN[:, sq_slot(k), :], X[:, k, :], ACT.Square).then_inc(sq_ready, 1)

            def norm_root(l, n):
                act.wait_ge(norm_mm, START + l * 2 + n + 1)
                act.activation(NR[:, 0:4], bank[4][:, 0:4], ACT.Sqrt, scale=1.0 / D, bias=eps_col).then_inc(rs_done, 1)

            def splits_and_squares(l, u0, norm_l, norm_n):
                for d in range(DT_):
                    if d >= 1:
                        act.wait_ge(bank_free[(u0 + d - 1) % 4], START + l * NBK + (u0 + d - 1) // 4 + 1)
                        norm_square(norm_l, norm_n, d - 1)
                    if d < DT_ - 1:
                        next_split(l, u0 + d)
                load_sqrt()
                act.wait_ge(bank_free[(u0 + 7) % 4], START + l * NBK + (u0 + 7) // 4 + 1)
                norm_square(norm_l, norm_n, 7)
                next_split(l, u0 + 7)

            def h_split(l, n0, src, tiles=range(KT)):
                for k in tiles:
                    act.wait_ge(hn_ready, l * 24 + n0 + k + 1)
                    act.activation(H[:, k, 0, :], src(k), ACT.Copy).then_inc(h_hi, 1)

            def square(l, b0, j, src, buf, depth=2):
                if j >= depth:
                    act.wait_ge(rn_mm, l * 16 + b0 + j + 1 - depth)
                act.activation(buf, src, ACT.Square).then_inc(rn_sq, 1)

            def rows_root(l, b0, n):
                act.wait_ge(rn_mm, l * 16 + b0 + n)
                cols_in, cols_out = (t[:, 0:4 * n].rearrange("p (c n) -> p c n", n=n) for t in (bank[4], NR))
                if n == 8:
                    act.activation(cols_out[:, :, 0:4], cols_in[:, :, 0:4], ACT.Sqrt, scale=float(P),
                                   bias=CO[:, C_MISC + 1:C_MISC + 2])
                    act.activation(cols_out[:, :, 4:8], cols_in[:, :, 4:8], ACT.Sqrt,
                                   bias=CO[:, C_MISC + 2:C_MISC + 3]).then_inc(rn_rs, 1)
                else:
                    act.activation(cols_out, cols_in, ACT.Sqrt, scale=1.0 / P, bias=eps_col).then_inc(rn_rs, 1)

            act.wait_ge(rot_v, 13)
            act.activation(CS[:, 1, :], TM[1][:, :], ACT.Sin).then_inc(rot_a, 1)
            act.activation(TM[2][:, :], TM[1][:, :], ACT.Sin, scale=0.5).then_inc(rot_a, 1)
            for k in range(KT):
                if k % 4 == 0:
                    act.wait_ge(ld_x[k // 4], 16)
                norm_square(0, 0, k)
            with act.Fori(0, L) as l:
                norm_root(l, 0)
                split_hi(l, 0)
                split_hi(l, 1)
                act.wait_ge(ld_mp, l * 16 + 16)
                act.activation(WAB[:, 0, :, :].rearrange("p a b -> p (a b)"), MP[:, M_WAB:M_WAB + 64],
                               ACT.Copy).then_inc(wab_hi, 1)
                h_split(l, 0, lambda k: HN[:, k, :])
                next_split(l, 0)

                act.wait_ge(ab_mm, l + 1)
                act.activation(ROW[0:8, :], bank[5][0:8, :], ACT.Copy).then_inc(ab_row, 1)
                next_split(l, 1)
                ab = bank[5][:, 0:32].rearrange("p (c n) -> p c n", n=8)
                act.wait_ge(ab_done, l + 1)
                act.activation(TB.rearrange("p (c h) -> p c h", h=4), ab[:, :, 4:8], ACT.Tanh, scale=0.5)\
                   .then_inc(sm_a, 1)
                act.activation(EA, MP[:, M_ALOG:M_ALOG + 4], ACT.Exp).then_inc(sm_a, 1)
                act.wait_ge(sm_v, l * 17 + 3)
                act.activation(EX, AX, ACT.Exp, scale=-1.0).then_inc(sm_a, 1)
                act.wait_ge(sm_a, l * 7 + 3)
                act.activation(LW, EX, ACT.Ln, bias=CO[:, C_ONE:C_ONE + 1]).then_inc(sm_a, 1)
                next_split(l, 2)

                def qk_square(j):
                    act.wait_ge(silu_done, l * 12 + j + 1)
                    square(l, 0, j, QTT[:, j, :] if j < 4 else KTT[:, j - 4, :], qk_sq(j), 4)

                def conv(u):
                    done(l, u)
                    if u >= 2:
                        act.wait_ge(silu_done, l * 12 + u - 1)
                    act.activation(TM[u % 2][:, :], bank[u % 4][:, :], ACT.Identity,
                                   scale=col(MP, M_CW + u * 4 + 3)).then_inc(cv_ready, 1)
                    if 1 <= u < 9:
                        qk_square(u - 1)
                    act.wait_ge(bank_free[u % 4], START + l * NBK + u // 4 + 1)
                    act.activation(TM[2 + u % 2][:, :], TM[u % 2][:, :], ACT.Tanh, scale=0.5).then_inc(th_ready, 1)

                conv(0)
                next_split(l, 3)
                act.wait_ge(sm_v, l * 17 + 15)
                act.activation(EGC, GCS[:, 0:16], ACT.Exp).then_inc(sm_a, 1)
                act.activation(EGT, GCS[:, 16:32], ACT.Exp).then_inc(sm_a, 1)
                act.wait_ge(sm_v, l * 17 + 16)
                act.activation(EKD, DL, ACT.Exp).then_inc(sm_a, 1)

                for u in range(1, 12):
                    if u == 3:
                        next_split(l, 4)
                    elif u >= 5:
                        next_split(l, u)
                    conv(u)
                    if u == 9:
                        rows_root(l, 0, 8)

                def silu_tanh(u, nth):
                    done(l, u)
                    if nth >= 2:
                        act.wait_ge(bank_free[(u - 2) % 4], START + l * NBK + (u - 2) // 4 + 1)
                    act.activation(TM[2 + u % 2][:, :], bank[u % 4][:, :], ACT.Tanh, scale=0.5).then_inc(zt_ready, 1)

                def fill(n):
                    u = U_CX + n
                    if n >= 1:
                        next_split(l, u)
                    if n < 4:
                        done(l, u)
                        act.activation(XC[n][:, :], bank[u % 4][:, :], ACT.Identity, scale=col(MP, M_LW + n * 4 + 3),
                                       bias=col(MP, M_LB + n)).then_inc(xc_ready, 1)
                    else:
                        silu_tanh(u, n - 4)

                fill(0)

                def prep_1(c):
                    i = l * NC + c
                    act.wait_ge(grow_done, i + 1)
                    if c >= 2:
                        act.wait_ge(qd_ready, i - 1)
                    act.activation(EG[:, c % 2, :], pb(c, 1), ACT.Exp).then_inc(eg_ready, 1)
                    act.wait_ge(el_pre, i + 1)
                    act.activation(EL[:, c % 2, :], EL[:, c % 2, :], ACT.Exp, scale=-1.0).then_inc(el_ready, 1)
                    act.wait_ge(tv_done, i + 1)
                    for h in range(NH):
                        last = act.activation(VB[:, c, h * P:(h + 1) * P], pb(c, 0)[:, h * P:(h + 1) * P], ACT.Copy,
                                              scale=col(HB, c * 4 + h))
                    last.then_inc(vb_ready, 1)

                def prep_2(c):
                    i = l * NC + c
                    act.wait_ge(tl_done, i + 1)
                    act.activation(LT[:, c, :], pb(c, 1), ACT.Copy).then_inc(lt_ready, 1)
                    act.wait_ge(tk_done, i + 1)
                    for h in range(NH):
                        last = act.activation(KD[:, c, h * P:(h + 1) * P], pb(c, 0)[:, h * P:(h + 1) * P], ACT.Copy,
                                              scale=col(EKD, c * 4 + h))
                    last.then_inc(kd_ready, 1)

                prep_1(0)
                prep_1(1)
                prep_2(0)
                prep_1(2)
                prep_2(1)
                prep_1(3)
                prep_2(2)
                prep_2(3)
                next_split(l, U_CX)

                for n in range(20):
                    act.wait_ge(t_done, l * 20 + n + 1)
                    act.activation(DTT[:, n % 4, :], bank[7][:, :], ACT.Copy).then_inc(dt_upd, 1)

                for c in range(NC):
                    i = l * NC + c
                    if c >= 1:
                        fill(2 * c)
                    act.wait_ge(vn_done, i + 1)
                    if c >= 1:
                        act.wait_ge(o_done, i)
                    act.activation(VN[:, :], bank[5][:, :], ACT.Copy).then_inc(vn_ready, 1)
                    fill(2 * c + 1)
                    act.wait_ge(o_done, i + 1)
                    act.activation(OT[:, :, chunk(c)], heads(bank[6][:, :]), ACT.Copy).then_inc(o_ready, 1)

                load_sqrt()
                act.wait_ge(bank_free[3], START + l * NBK + 5)
                act.wait_ge(o_ready, l * NC + 4)
                for j in range(4):
                    square(l, 8, j, OT[:, j, :], SQ[j % 2][:, :])
                rows_root(l, 8, 4)

                def y_split(nth, t, src):
                    act.wait_ge(y_fin, l * 12 + nth + 1)
                    act.activation(Y[:, t, 0, :], src, ACT.Copy).then_inc(y_hi, 1)

                for i in range(4):
                    u = U_BQK + i
                    next_split(l, u)
                    done(l, u)
                    act.activation(RAW[:, i, :], bank[u % 4][:, :], ACT.Copy).then_inc(raw_ready, 1)
                    act.wait_ge(lru_mm, l * 4 + i + 1)
                    act.activation(TH[:, i, :], bank[lru_bank(i)][:, :], ACT.Tanh, scale=0.5, bias=col(HBA, i))
                    act.activation(TI[:, i, :], bank[lru_bank(i) + 1][:, :], ACT.Tanh, scale=0.5,
                                   bias=col(HBA, 4 + i)).then_inc(lru_t, 1)
                    act.wait_ge(lru_t, l * 4 + i + 1)
                    act.activation(TH[:, i, :], TH[:, i, :], ACT.Tanh, scale=col(SP2, i), bias=col(SP2, i))\
                       .then_inc(lru_th, 1)
                next_split(l, U_CG)
                for i in range(4):
                    y_split(i, i, OT[:, i, :])
                for j in range(4):
                    act.wait_ge(lru_v, l * 28 + j * 5 + 1)
                    act.activation(TH[:, j, :], TH[:, j, :], ACT.Sqrt).then_inc(lru_sq, 1)

                def gelu_1(j):
                    u = U_CG + j
                    if j >= 1:
                        next_split(l, u)
                    done(l, u)
                    if j >= 2:
                        act.wait_ge(y_fin, l * 12 + 4 + j - 1)
                    else:
                        act.wait_ge(rq_ready, l * 4 + 4)
                    act.activation(TM[j % 2][:, :], bank[u % 4][:, :], ACT.Square).then_inc(ge_a, 1)

                def gelu_2(j):
                    act.wait_ge(ge_v, l * 8 + 2 * j + 2)
                    act.activation(TM[j % 2][:, :], TM[j % 2][:, :], ACT.Tanh, scale=0.7978845608028654)\
                       .then_inc(ge_t, 1)

                gelu_1(0)
                gelu_1(1)
                gelu_2(0)
                for j in range(4):
                    y_split(4 + j, 8 + j, TM[4 + j % 2][:, :])
                    if j + 2 < 4:
                        gelu_1(j + 2)
                    if j + 1 < 4:
                        gelu_2(j + 1)

                def bv_out(h):
                    act.wait_ge(bvt_done, l * 4 + h + 1)
                    act.activation(BV[:, h, :], bank[4 + h % 2][:, :], ACT.Copy).then_inc(bv_ready, 1)

                for h in range(NH):
                    u = U_BV + h
                    next_split(l, u)
                    done(l, u)
                    act.wait_ge(perm_done, l * 4 + 4)
                    act.activation(RAW[:, h, :], bank[u % 4][:, :], ACT.Copy).then_inc(bank_free[u % 4], 1)
                    if h >= 2:
                        bv_out(h - 2)

                def bg_tanh(h):
                    next_split(l, U_BG + h)
                    silu_tanh(U_BG + h, h)

                bv_out(2)
                bg_tanh(0)
                bv_out(3)

                def retention_out(h):
                    act.wait_ge(pv_done, l * 4 + h + 1)
                    act.activation(OB[:, h, :], bank[7][:, :], ACT.Copy).then_inc(ob_ready, 1)

                bg_tanh(1)
                bg_tanh(2)
                retention_out(0)
                bg_tanh(3)
                for h in range(1, NH):
                    retention_out(h)

                for u in (U_BG + 2, U_BG + 3):
                    act.wait_ge(bank_free[u % 4], START + l * NBK + u // 4 + 1)
                load_sqrt()
                next_split(l, U_MIX)
                for j in range(4):
                    act.wait_ge(cen_ready, l * 4 + j + 1)
                    square(l, 12, j, OB[:, j, :], SQ[j % 2][:, :])

                for d in range(DT_):
                    for n in range(4):
                        u = U_MIX + 4 * d + n
                        if u > U_MIX:
                            next_split(l, u)
                        if d == 0 and n == 0:
                            rows_root(l, 12, 4)
                        if n < 3:
                            done(l, u)
                            if d >= 2:
                                act.wait_ge(mg_done, l * 8 + d - 1)
                            act.activation(GT[:, d % 2, n, :], bank[n][:, :], ACT.Tanh, scale=0.5)\
                               .then_inc(bank_free[n], 1)
                        if d == DT_ - 1 and n == 2:
                            h_split(l, 8, lambda k: MM[:, k, :], range(7))
                        if d == 0 and n == 2:
                            for h in range(4):
                                if h == 2:
                                    act.wait_ge(y_fin, l * 12 + 12)
                                y_split(8 + h, 4 + h, OB[:, h, :])
                h_split(l, 8, lambda k: MM[:, k, :], range(7, 8))
                splits_and_squares(l, U_OUT, l, 1)
                norm_root(l, 1)
                h_split(l, 16, lambda k: HN[:, k, :])

                act.wait_ge(ld_fp, l * 16 + 16)
                p0 = 0
                for g in range(2):
                    for i in range(PAIRS[g]):
                        p, u = p0 + i, U_FFN[g] + 2 * i
                        next_split(l, u)
                        done(l, u)
                        if p >= 2:
                            act.wait_ge(fg_done, l * 22 + p - 1)
                        act.activation(CG[:, p % 2, :], bank[u % 4][:, :], ACT.Identity, scale=col(FP, F_W + p * 3 + 2),
                                       bias=col(FP, F_B + p)).then_inc(fc_ready, 1)
                        act.wait_ge(bank_free[u % 4], START + l * NBK + u // 4 + 1)
                        act.activation(TG[:, p % 2, :], CG[:, p % 2, :], ACT.Tanh, scale=0.5).then_inc(ft_ready, 1)
                        next_split(l, u + 1)
                        done(l, u + 1)
                        if p >= 2:
                            act.wait_ge(f_lo, START + l * 22 + p - 1)
                        act.activation(CV[:, p % 2, :], bank[(u + 1) % 4][:, :], ACT.Identity,
                                       scale=col(FP, F_W + (22 + p) * 3 + 2), bias=col(FP, F_B + 22 + p))\
                           .then_inc(fc_ready, 1)
                        act.wait_ge(fg_done, l * 22 + p + 1)
                        act.activation(Y[:, i, 0, :], CV[:, p % 2, :], ACT.Copy).then_inc(f_hi, 1)
                    if g == 0:
                        for d in range(DT_):
                            next_split(l, U_DOWN[0] + d)
                    else:
                        splits_and_squares(l, U_DOWN[1], l + 1, 0)
                    p0 += PAIRS[g]
            norm_root(L, 0)

        @block.gpsimd
        def _(pool):
            def split_lo(l, u):
                pool.wait_ge(w_hi, l * NU + u + 1)
                n = unit_k(u) * P
                pool.tensor_tensor(SPL[:, u % 2, 1, 0:n], STG[:, u % NST, 0:n], SPL[:, u % 2, 0, 0:n], SUB)\
                    .then_inc(w_lo, 1)

            def h_rest(l, batch, src, tiles=range(1, KT, 2)):
                for k in tiles:
                    pool.wait_ge(h_hi, l * 24 + 8 * batch + k + 1)
                    pool.tensor_tensor(H[:, k, 1, :], src[:, k, :], H[:, k, 0, :], SUB).then_inc(h_lo[1], 1)

            pool.memset(SM[:, 396:397], 0.0).then_inc(w_lo, 1)
            with pool.Fori(0, L) as l:
                split_lo(l, 0)
                split_lo(l, 1)
                pool.wait_ge(wab_hi, l + 1)
                pool.tensor_tensor(WAB[:, 1, :, :].rearrange("p a b -> p (a b)"), MP[:, M_WAB:M_WAB + 64],
                                   WAB[:, 0, :, :].rearrange("p a b -> p (a b)"), SUB).then_inc(wab_lo, 1)
                h_rest(l, 0, HN)
                for u in range(2, 14):
                    split_lo(l, u)
                for c in range(NC):
                    i = l * NC + c
                    pool.wait_ge(eg_ready, i + 1)
                    pool.wait_ge(qk_done, i + 1)
                    pool.tensor_tensor(QTT[:, :, chunk(c)], QTT[:, :, chunk(c)], heads(EG[:, c % 2, :]), MUL)\
                        .then_inc(qd_ready, 1)
                    pool.wait_ge(lt_ready, i + 1)
                    pool.tensor_tensor(heads(DTT[:, c, :]), heads(LT[:, c, :]), over_heads(neg_m1t), MUL)\
                        .then_inc(dt_pre, 1)
                    pool.wait_ge(dt_pre, i + 1)
                    pool.tensor_tensor(heads(DTT[:, c, :]), heads(DTT[:, c, :]), over_heads(ident), ADD)\
                        .then_inc(dt_init, 1)
                for u in range(14, NU):
                    split_lo(l, u)
                    if u == U_OUT:
                        h_rest(l, 1, MM, range(1, 6, 2))
                    if u == U_OUT + 1:
                        h_rest(l, 1, MM, range(7, 8))
                    if u == U_FFN[0] + 1:
                        h_rest(l, 2, HN)

        @block.tensor
        def _(pe):
            def product(l, u, dst, k0, src, nk=None, last_signal=True, arrives=None, beside=None):
                nk = unit_k(u) if nk is None else nk
                for k in range(nk):
                    if arrives is not None:
                        arrives(k)
                    w = [SPL[:, u % 2, part, (k0 + k) * P:(k0 + k + 1) * P] for part in range(2)]
                    for n, (a, b) in enumerate(((0, 0), (0, 1), (1, 0))):
                        mm = pe.matmul(dst, w[a], src(k0 + k)[:, b, :], start=(k == 0 and n == 0),
                                       stop=(k == nk - 1 and n == 2))
                    if beside is not None:
                        beside(k)
                if last_signal:
                    mm.then_inc(gemm_done, 1)

            def h_part(k):
                return H[:, k, :, :]

            def y_part(k):
                return Y[:, k, :, :]

            def gemm(l, u, src=h_part, arrives=None, beside=None):
                pe.wait_ge(w_lo, START + l * NU + u + 1)
                pe.wait_ge(bank_free[u % 4], START + l * NBK + u // 4)
                product(l, u, bank[u % 4][:, :], 0, src, arrives=arrives, beside=beside)

            def h_arrives(l, batch):
                return lambda k: pe.wait_ge(h_lo[k % 2], l * 12 + 4 * batch + k // 2 + 1)

            def norm_sum(l, n):
                pe.wait_ge(sq_sum, l * 12 + n * 6 + 6)
                pe.wait_ge(sq_ready, l * 16 + n * 8 + 8)
                for c in range(NC):
                    for slot in (0, sq_slot(7)):
                        mm = pe.matmul(bank[4][:, c:c + 1], SQN[:, slot, chunk(c)], ones[:, 0:1],
                                       start=(slot == 0), stop=(slot != 0))
                mm.then_inc(norm_mm, 1)

            def norm_broadcast(l, n):
                pe.wait_ge(ri_done, l * 2 + n + 1)
                pe.matmul(bank[7][0:4, 0:P], NI[:, 0:4], ident, start=True, stop=True).then_inc(nt_done, 1)
                pe.wait_ge(nt_row, l * 2 + n + 1)
                for c in range(NC):
                    mm = pe.matmul(bank[6][:, chunk(c)], CO[0:4, C_ID + c:C_ID + c + 1].to_broadcast([4, P]),
                                   ROWI[0:4, 0:P], start=True, stop=True)
                mm.then_inc(nb_done, 1)

            def row_sum(l, b0, j, n, buf):
                pe.wait_ge(rn_sq, l * 16 + b0 + j + 1)
                for c in range(NC):
                    mm = pe.matmul(bank[4][:, c * n + j:c * n + j + 1], buf[:, chunk(c)], ones[:, 0:1],
                                   start=True, stop=True)
                mm.then_inc(rn_mm, 1)

            def rows_turn(l, n, nth):
                pe.wait_ge(rn_ri, l * 3 + nth + 1)
                pe.matmul(bank[7][0:4 * n, 0:P], NI[:, 0:4 * n], ident, start=True, stop=True).then_inc(rn_tp, 1)

            def row_broadcast(l, b0, rows, nth, n=8):
                pe.wait_ge(rn_tr, l * 3 + nth + 1)
                for j in rows:
                    depth = 4 if b0 == 0 else 2
                    if j >= depth:
                        pe.wait_ge(rn_app, l * 16 + b0 + j + 1 - depth)
                    for c in range(NC):
                        row = C_ID + c * n + j
                        mm = pe.matmul(row_bank(b0, j)[:, chunk(c)], CO[0:4 * n, row:row + 1].to_broadcast([4 * n, P]),
                                       ROWI[0:4 * n, 0:P], start=True, stop=True)
                    mm.then_inc(rn_b, 1)

            pe.wait_ge(ld_const, 32)
            pe.matmul(bank[7][:, 0:2], ident, ident[:, 0:2], start=True, stop=True).then_inc(gemm_done, 1)
            pe.matmul(bank[7][:, 0:2], ident, ident[:, 0:2], start=True, stop=True).then_inc(norm_mm, 1)
            norm_sum(0, 0)
            with pe.Fori(0, L) as l:
                norm_broadcast(l, 0)

                def alpha_beta(k):
                    if k == 0:
                        pe.wait_ge(wab_lo, l + 1)
                    for n, (a, b) in enumerate(((0, 0), (1, 0), (0, 1))):
                        mm = pe.matmul(bank[5][0:8, :], WAB[:, b, k, :], H[:, k, a, :],
                                       start=(k == 0 and n == 0), stop=(k == KT - 1 and n == 2))
                    if k == KT - 1:
                        mm.then_inc(ab_mm, 1)

                gemm(l, 0, arrives=h_arrives(l, 0), beside=alpha_beta)
                gemm(l, 1)
                pe.wait_ge(ab_row, l + 1)
                for c in range(NC):
                    mm = pe.matmul(bank[5][:, c * 8:c * 8 + 8], ROW[0:8, chunk(c)], ident[0:8, 0:8],
                                   start=True, stop=True)
                mm.then_inc(ab_done, 1)
                gemm(l, 2)
                gemm(l, 3)
                pe.wait_ge(sm_v, l * 17 + 14)
                pe.matmul(bank[5][:, 64:80], upper, GG, start=True, stop=True)
                pe.matmul(bank[5][:, 80:96], ones, GG, start=True, stop=True).then_inc(gc_done, 1)
                for u in range(4, 12):
                    gemm(l, u)
                    for j in ((0,), (1, 2), (3, 4), (5,), (6,), (7,), (), ())[u - 4]:
                        row_sum(l, 0, j, 8, qk_sq(j))
                    if u == 10:
                        rows_turn(l, 8, 0)
                        row_broadcast(l, 0, range(4), 0)
                row_broadcast(l, 0, range(4, 8), 0)
                gemm(l, U_CX)

                def prep_1(c):
                    i = l * NC + c
                    pe.wait_ge(ug_ready, i + 1)
                    if c >= 2:
                        pe.wait_ge(lt_ready, i - 1)
                        pe.wait_ge(att_ready, i - 1)
                        pe.wait_ge(kd_ready, i - 1)
                    if c == 0:
                        pe.wait_ge(rn_app, l * 16 + 6)
                    if c == 1:
                        pe.wait_ge(silu_done, l * 12 + 12)
                    pe.matmul(pb(c, 1), ones, TM[c % 2][:, :], start=True, stop=True).then_inc(grow_done, 1)
                    if c == 0:
                        pe.wait_ge(rn_app, l * 16 + 8)
                        pe.wait_ge(silu_done, l * 12 + 12)
                    for h in range(NH):
                        k_c = KTT[:, h, chunk(c)]
                        mm = pe.matmul(pb(c, 2)[:, h * P:(h + 1) * P], k_c, k_c, start=True, stop=True)
                    mm.then_inc(kk_done, 1)
                    for h in range(NH):
                        mm = pe.matmul(pb(c, 3)[:, h * P:(h + 1) * P], QTT[:, h, chunk(c)], KTT[:, h, chunk(c)],
                                       start=True, stop=True)
                    mm.then_inc(qk_done, 1)
                    if c == 1:
                        pe.wait_ge(bank_free[U_CX % 4], START + l * NBK + U_CX // 4 + 1)
                    for h in range(NH):
                        mm = pe.transpose(pb(c, 0)[:, h * P:(h + 1) * P], VT[:, h, chunk(c)], ident)
                    mm.then_inc(tv_done, 1)

                def prep_2(c):
                    i = l * NC + c
                    pe.wait_ge(l_ready, i + 1)
                    pe.wait_ge(eg_ready, i + 1)
                    for h in range(NH):
                        mm = pe.transpose(pb(c, 1)[:, h * P:(h + 1) * P], DD[:, c, h * P:(h + 1) * P], ident)
                    mm.then_inc(tl_done, 1)
                    pe.wait_ge(at_ready, i + 1)
                    for h in range(NH):
                        mm = pe.transpose(pb(c, 2)[:, h * P:(h + 1) * P], TM[2 + c % 2][:, h * P:(h + 1) * P], ident)
                    mm.then_inc(ta_done, 1)
                    pe.wait_ge(vb_ready, i + 1)
                    for h in range(NH):
                        mm = pe.transpose(pb(c, 0)[:, h * P:(h + 1) * P], KTT[:, h, chunk(c)], ident)
                    mm.then_inc(tk_done, 1)

                prep_1(0)
                prep_1(1)
                prep_2(0)
                prep_1(2)
                prep_2(1)
                prep_1(3)
                prep_2(2)
                prep_2(3)

                def level_y(n):
                    c = n % 4
                    if n < 4:
                        pe.wait_ge(d_init, l * 4 + c + 1)
                        if n == 0:
                            pe.wait_ge(att_ready, l * 4 + 4)
                            pe.wait_ge(kd_ready, l * 4 + 4)
                            pe.wait_ge(lt_ready, l * 4 + 4)
                    else:
                        pe.wait_ge(d_upd, l * 20 + n - 3)
                    if n >= 2:
                        pe.wait_ge(ym_ready, l * 24 + n - 1)
                    for h in range(NH):
                        s = slice(h * P, (h + 1) * P)
                        mm = pe.matmul(bank[4 + n % 2][:, s], LT[:, c, s], DD[:, c, s], start=True, stop=True)
                    mm.then_inc(y_done, 1)

                def level_t(n):
                    pe.wait_ge(d_upd, l * 20 + n + 1)
                    if n >= 1:
                        pe.wait_ge(dt_upd, l * 20 + n)
                    for h in range(NH):
                        s = slice(h * P, (h + 1) * P)
                        mm = pe.transpose(bank[7][:, s], DD[:, n % 4, s], ident)
                    mm.then_inc(t_done, 1)

                level_y(0)
                for n in range(24):
                    if n + 1 < 24:
                        level_y(n + 1)
                    c = n % 4
                    if n == 20:
                        level_t(19)
                        pe.wait_ge(dt_upd, l * 20 + 20)
                    pe.wait_ge(ym_ready, l * 24 + n + 1)
                    if n < 4:
                        pe.wait_ge(dt_init, l * 4 + c + 1)
                    elif n < 20:
                        pe.wait_ge(dt_upd, l * 20 + n - 3)
                    if 1 <= n < 20:
                        pe.wait_ge(d_upd, l * 20 + n)
                    if n >= 21:
                        pe.wait_ge(dt_fin, l * 4 + n - 20)
                    for h in range(NH):
                        s = slice(h * P, (h + 1) * P)
                        if n < 20:
                            mm = pe.matmul(bank[6][:, s], DTT[:, c, s], YM[:, n % 2, s], start=True, stop=True)
                        else:
                            mm = pe.matmul(bank[7][:, s], YM[:, n % 2, s], DTT[:, c, s], start=True, stop=True)
                    mm.then_inc(p_done, 1)
                    if 1 <= n < 20:
                        level_t(n - 1)

                pe.wait_ge(dt_fin, l * 4 + 4)
                pe.wait_ge(qd_ready, l * 4 + 4)
                for c in range(NC):
                    i = l * NC + c
                    if c >= 1:
                        pe.wait_ge(s_upd, l * 3 + c)
                        for h in range(NH):
                            s = slice(h * P, (h + 1) * P)
                            mm = pe.matmul(bank[4][:, s], KTT[:, h, chunk(c)], ST[c % 2][:, s], start=True, stop=True)
                        mm.then_inc(ks_done, 1)
                    if c >= 1:
                        gemm(l, U_CX + 2 * c)
                    if c >= 1:
                        pe.wait_ge(r_ready, l * 3 + c)
                    for h in range(NH):
                        s = slice(h * P, (h + 1) * P)
                        mm = pe.matmul(bank[5][:, s], DTT[:, c, s], (RR[:, s] if c else VB[:, 0, s]),
                                       start=True, stop=True)
                    mm.then_inc(vn_done, 1)
                    gemm(l, U_CX + 2 * c + 1)
                    pe.wait_ge(vn_ready, i + 1)
                    if c < NC - 1:
                        for h in range(NH):
                            s = slice(h * P, (h + 1) * P)
                            mm = pe.matmul(bank[7][:, s], KD[:, c, s], VN[:, s], start=True, stop=True)
                        mm.then_inc(su_done, 1)
                    if c >= 1:
                        pe.wait_ge(o_ready, i)
                    for h in range(NH):
                        s = slice(h * P, (h + 1) * P)
                        mm = pe.matmul(bank[6][:, s], VN[:, s], ATT[:, c, s], start=True, stop=(c == 0))
                        if c >= 1:
                            mm = pe.matmul(bank[6][:, s], ST[c % 2][:, s], QTT[:, h, chunk(c)], start=False, stop=True)
                    mm.then_inc(o_done, 1)

                gemm(l, U_BQK)
                for j in range(4):
                    row_sum(l, 8, j, 4, SQ[j % 2][:, :])
                gemm(l, U_BQK + 1)
                rows_turn(l, 4, 1)

                def lru_gates(j):
                    u = U_CX + j
                    pe.wait_ge(bank_free[u % 4], START + l * NBK + u // 4 + 1)
                    if j == 0:
                        pe.wait_ge(rn_rs, l * 3 + 2)
                    elif j == 1:
                        pe.wait_ge(rn_app, l * 16 + 12)
                    else:
                        pe.wait_ge(lru_t, l * 4 + j - 1)
                    b = lru_bank(j)
                    pe.matmul(bank[b][:, :], MP[:, M_WA + j * P:M_WA + (j + 1) * P], XC[j][:, :], start=True, stop=True)
                    pe.matmul(bank[b + 1][:, :], MP[:, M_WX + j * P:M_WX + (j + 1) * P], XC[j][:, :],
                              start=True, stop=True).then_inc(lru_mm, 1)

                lru_gates(0)
                row_broadcast(l, 8, range(4), 1, 4)
                gemm(l, U_BQK + 2)
                lru_gates(1)
                gemm(l, U_BQK + 3)
                lru_gates(2)
                lru_gates(3)

                def rotate(i):
                    pe.wait_ge(raw_ready, l * 4 + i + 1)
                    if i < 2:
                        pe.wait_ge(lru_t, l * 4 + 3)
                    else:
                        pe.wait_ge(rot_m2, l * 4 + i - 1)
                    pe.matmul(bank[4 + i % 2][:, :], perm, RAW[:, i, :], start=True, stop=True)\
                      .then_inc(perm_done, 1)

                gemm(l, U_CG)
                rotate(0)
                rotate(1)
                gemm(l, U_CG + 1)
                rotate(2)
                rotate(3)
                gemm(l, U_CG + 2)
                gemm(l, U_CG + 3)

                def turn_v(h):
                    pe.wait_ge(bank_free[(U_BV + h) % 4], START + l * NBK + (U_BV + h) // 4 + 1)
                    if h < 2:
                        pe.wait_ge(rot_m2, l * 4 + h + 3)
                    else:
                        pe.wait_ge(bv_ready, l * 4 + h - 1)
                    for c in range(NC):
                        mm = pe.transpose(bank[4 + h % 2][:, chunk(c)], RAW[:, h, chunk(c)], ident)
                    mm.then_inc(bvt_done, 1)

                def scores(h, j):
                    r = slice(64 * (h % 2), 64 * (h % 2) + 64)
                    n = h * 4 + j
                    if n >= 3:
                        pe.wait_ge(sc_ready, l * 16 + n - 2)
                    if n in (1, 2):
                        pe.wait_ge(bv_ready, l * 4 + n + 2)
                    pe.matmul(score_bank(n)[:, 0:T - j * P], RQ[r, 2 + h // 2, chunk(j)],
                              RQ[r, h // 2, j * P:T], start=True, stop=True).then_inc(sc_done, 1)

                def values(h):
                    pe.wait_ge(sc_ready, l * 16 + 4 * h + 4)
                    if h >= 1:
                        pe.wait_ge(ob_ready, l * 4 + h)
                    off = 0
                    for j in range(NC):
                        mm = pe.matmul(bank[7][:, j * P:T], BV[:, h, chunk(j)], SC[h % 2][:, off:off + T - j * P],
                                       start=(j == 0), stop=(j == NC - 1), skip_group_check=True)
                        off += T - j * P
                    mm.then_inc(pv_done, 1)

                gemm(l, U_BV)
                gemm(l, U_BV + 1)
                turn_v(0)
                gemm(l, U_BV + 2)
                turn_v(1)
                gemm(l, U_BV + 3)
                turn_v(2)
                gemm(l, U_BG)
                turn_v(3)
                pe.wait_ge(ld_dm, l * 16 + 16)
                pe.wait_ge(rq_ready, l * 4 + 4)
                for j in range(3):
                    scores(0, j)
                gemm(l, U_BG + 1)
                scores(0, 3)
                for j in range(2):
                    scores(1, j)
                gemm(l, U_BG + 2)
                values(0)
                for j in range(2, 4):
                    scores(1, j)
                scores(2, 0)
                gemm(l, U_BG + 3)
                values(1)
                for j in range(1, 4):
                    scores(2, j)
                values(2)
                for j in range(4):
                    scores(3, j)
                gemm(l, U_MIX)
                values(3)
                for h in range(NH):
                    pe.wait_ge(ob_ready, l * 4 + h + 1)
                    if h >= 2:
                        pe.wait_ge(cen_ready, l * 4 + h - 1)
                    pe.matmul(bank[5 + h % 2][:, :], ones, OB[:, h, :], start=True, stop=True).then_inc(mean_done, 1)
                gemm(l, U_MIX + 1)
                for j in range(4):
                    row_sum(l, 12, j, 4, SQ[j % 2][:, :])
                gemm(l, U_MIX + 2)

                for d in range(DT_):
                    if d >= 1:
                        for n in range(3):
                            gemm(l, U_MIX + 4 * d + n)
                    u = U_MIX + 4 * d + 3
                    if d == 0:
                        pe.wait_ge(y_lo, l * 12 + 8)
                    pe.wait_ge(w_lo, START + l * NU + u + 1)
                    pe.wait_ge(bank_free[3], START + l * NBK + u // 4)
                    if d >= 1:
                        pe.wait_ge(mg_done, l * 8 + d)
                    for n in (0, 2, 1):
                        if d == 0 and n == 1:
                            rows_turn(l, 4, 2)
                            row_broadcast(l, 12, range(4), 2, 4)
                        product(l, u, bank[3 + n][:, :], 4 * n, y_part, nk=4, last_signal=(n == 1),
                                arrives=(lambda k: pe.wait_ge(y_lo, l * 12 + 9 + k)) if d == 0 and n == 1 else None)
                for d in range(DT_):
                    gemm(l, U_OUT + d, arrives=h_arrives(l, 1) if d == 0 else None)
                norm_sum(l, 1)
                norm_broadcast(l, 1)
                for g in range(2):
                    for i in range(2 * PAIRS[g]):
                        gemm(l, U_FFN[g] + i, arrives=h_arrives(l, 2) if g == 0 and i == 0 else None)
                    p0 = 0 if g == 0 else PAIRS[0]
                    for d in range(DT_):
                        gemm(l, U_DOWN[g] + d, y_part,
                             arrives=(lambda k: pe.wait_ge(f_lo, START + l * 22 + p0 + k + 1)) if d == 0 else None)
                norm_sum(l + 1, 0)
            norm_broadcast(L, 0)

        @block.vector
        def _(dve):
            def shift_taps(l, u, dst, width, w0, ready, n_ready, acc, n_acc):
                b = bank[u % 4]
                dve.wait_ge(ready, n_ready)
                for s in range(1, width):
                    if s > 1:
                        dve.wait_ge(acc, n_acc + s - 1)
                    ins = dve.scalar_tensor_tensor(out=dst[:, s:T], in0=b[:, 0:T - s], scalar=w0(width - 1 - s),
                                                   in1=dst[:, s:T], op0=MUL, op1=ADD)
                    ins.then_inc(*((acc, 1) if s < width - 1 else (bank_free[u % 4], 1)))

            def h_rest(l, batch, k, src):
                dve.wait_ge(h_hi, l * 24 + 8 * batch + k + 1)
                dve.tensor_tensor(H[:, k, 1, :], src[:, k, :], H[:, k, 0, :], SUB).then_inc(h_lo[0], 1)

            def square_sum(l, n, k):
                dve.wait_ge(sq_ready, l * 16 + n * 8 + k + 1)
                if k >= 2:
                    dve.wait_ge(sq_sum, l * 12 + n * 6 + k - 1)
                dve.tensor_tensor(SQN[:, 0, :], SQN[:, 0, :], SQN[:, sq_slot(k), :], ADD).then_inc(sq_sum, 1)

            def norm_inverse(l, n):
                dve.wait_ge(rs_done, l * 2 + n + 1)
                dve.reciprocal(NI[:, 0:4], NR[:, 0:4]).then_inc(ri_done, 1)
                dve.wait_ge(nt_done, l * 2 + n + 1)
                dve.tensor_copy(ROWI[0:4, 0:P], bank[7][0:4, 0:P]).then_inc(nt_row, 1)
                dve.wait_ge(nb_done, l * 2 + n + 1)

            def norm_apply(l, n, g0, batch):
                norm_inverse(l, n)
                for k in range(KT):
                    dve.scalar_tensor_tensor(out=HN[:, k, :], in0=X[:, k, :], scalar=col(MP, g0 + k),
                                             in1=bank[6][:, :], op0=MUL, op1=MUL).then_inc(hn_ready, 1)
                    if k % 2 == 1:
                        h_rest(l, batch, k - 1, HN)

            def rows_inverse(l, n, nth):
                dve.wait_ge(rn_rs, l * 3 + nth + 1)
                dve.reciprocal(NI[:, 0:4 * n], NR[:, 0:4 * n]).then_inc(rn_ri, 1)
                dve.wait_ge(rn_tp, l * 3 + nth + 1)
                dve.tensor_copy(ROWI[0:4 * n, 0:P], bank[7][0:4 * n, 0:P]).then_inc(rn_tr, 1)

            n_rot = [0]

            def rot(ins):
                ins.then_inc(rot_v, 1)
                n_rot[0] += 1
                dve.wait_ge(rot_v, n_rot[0])

            for b in range(4):
                dve.memset(SM[:, 397 + b:398 + b], 0.0).then_inc(bank_free[b], 1)
            dve.memset(SM[:, 401:402], 0.0).then_inc(f_lo, 1)

            magic = 1.5 * 2.0 ** 23
            turn = (6.28125, 0.0019350051879882812, 3.019916050561733e-07)
            dve.wait_ge(ld_pos, 32)
            ang, cnt = TM[1][:, :], TM[2][:, :]
            rot(dve.tensor_copy(TM[3][:, :], TM[0][:, :].bitcast(I32)))
            rot(dve.tensor_scalar(ang, TM[3][:, :], CO[:, C_MISC:C_MISC + 1], None, MUL))
            for m in (4096.0, 1.0):
                rot(dve.tensor_scalar(cnt, ang, 1.0 / (2 * 3.141592653589793 * m), magic, MUL, ADD))
                rot(dve.tensor_scalar(cnt, cnt, magic, None, SUB))
                for part in turn:
                    rot(dve.scalar_tensor_tensor(out=ang, in0=cnt, scalar=-part * m, in1=ang, op0=MUL, op1=ADD))
            rot(dve.tensor_scalar(ang, ang, 3.1415925, -3.1415925, MIN, MAX))
            dve.wait_ge(rot_a, 2)
            rot_n = 13
            dve.tensor_tensor(TM[3][:, :], TM[2][:, :], TM[2][:, :], MUL).then_inc(rot_v, 1)
            dve.wait_ge(rot_v, rot_n + 1)
            dve.tensor_scalar(CS[:, 0, :], TM[3][:, :], -2.0, 1.0, MUL, ADD).then_inc(rot_v, 1)
            dve.wait_ge(rot_v, rot_n + 2)
            for k in range(1, 7):
                square_sum(0, 0, k)

            with dve.Fori(0, L) as l:
                dve.wait_ge(ld_mp, l * 16 + 16)
                norm_apply(l, 0, M_GA, 0)

                n_s = [0]

                def step(ins):
                    ins.then_inc(sm_v, 1)
                    n_s[0] += 1
                    dve.wait_ge(sm_v, l * 17 + n_s[0])

                ab = bank[5][:, 0:32].rearrange("p (c n) -> p c n", n=8)
                ch = "p (c h) -> p c h"
                dve.wait_ge(ab_done, l + 1)
                dve.wait_ge(sm_a, l * 7 + 1)
                step(dve.tensor_tensor(XS[:, 0:16].rearrange(ch, h=4), ab[:, :, 0:4],
                                       MP[:, M_DT:M_DT + 4].unsqueeze(1).to_broadcast([P, NC, 4]), ADD))
                step(dve.tensor_scalar(XS[:, 16:20], MP[:, M_LAM:M_LAM + 4], -1.0, None, MUL))
                step(dve.scalar_tensor_tensor(out=AX, in0=XS, scalar=-1.0, in1=XS, op0=MUL, op1=MAX))
                dve.wait_ge(sm_a, l * 7 + 4)
                step(dve.tensor_scalar(WM, EX, 1.0, 1.0, ADD, SUB))
                step(dve.tensor_scalar(WM, WM, 1e-30, None, MAX))
                step(dve.reciprocal(RC, WM))
                step(dve.tensor_tensor(RC, RC, EX, MUL))
                step(dve.tensor_tensor(RC, RC, LW, MUL))
                step(dve.scalar_tensor_tensor(out=SP, in0=XS, scalar=0.0, in1=RC, op0=MAX, op1=ADD))
                step(dve.tensor_scalar(SP2, SP[:, 16:20], 2.0, None, MUL))
                step(dve.tensor_scalar(BE, TB, 0.5, 0.5, MUL, ADD))
                step(dve.tensor_scalar(HB, BE, 0.5, None, MUL))
                step(dve.tensor_scalar(HBA, MP[:, M_BA:M_BA + 8], 0.5, None, MUL))
                step(dve.scalar_tensor_tensor(out=GG.rearrange(ch, h=4), in0=SP[:, 0:16].rearrange(ch, h=4),
                                              scalar=-1.0, in1=EA.unsqueeze(1).to_broadcast([P, NC, 4]),
                                              op0=MUL, op1=MUL))

                def silu_conv(u):
                    shift_taps(l, u, TM[u % 2], 4, lambda j: col(MP, M_CW + u * 4 + j), cv_ready, l * 12 + u + 1,
                               cv_acc, l * 24 + 2 * u)
                    dve.wait_ge(th_ready, l * 12 + u + 1)
                    dst = (QTT, KTT, VT)[u // 4][:, u % 4, :]
                    dve.scalar_tensor_tensor(out=dst, in0=TM[2 + u % 2][:, :], scalar=1.0, in1=TM[u % 2][:, :],
                                             op0=ADD, op1=MUL).then_inc(silu_done, 1)

                silu_conv(0)
                dve.wait_ge(gc_done, l + 1)
                step(dve.tensor_copy(GCS, bank[5][:, 64:96]))
                step(dve.tensor_tensor(DL, GCS[:, 16:32], GCS[:, 0:16], SUB))
                dve.wait_ge(sm_a, l * 7 + 7)
                step(dve.scalar_tensor_tensor(out=NBG, in0=BE, scalar=-1.0, in1=EGC, op0=MUL, op1=MUL))
                for u in range(1, 10):
                    silu_conv(u)
                rows_inverse(l, 8, 0)
                silu_conv(10)

                def l2_scale(j):
                    t = QTT[:, j, :] if j < 4 else KTT[:, j - 4, :]
                    dve.wait_ge(rn_b, l * 16 + j + 1)
                    dve.tensor_tensor(t, t, row_bank(0, j), MUL).then_inc(rn_app, 1)

                for j in range(4):
                    l2_scale(j)
                silu_conv(11)

                def cum_weights(c):
                    if c >= 2:
                        dve.wait_ge(grow_done, l * NC + c - 1)
                    for h in range(NH):
                        ins = dve.tensor_scalar(TM[c % 2][:, h * P:(h + 1) * P], upper, col(GG, c * 4 + h), None, MUL)
                    ins.then_inc(ug_ready, 1)

                dve.wait_ge(silu_done, l * 12 + 12)
                cum_weights(0)
                cum_weights(1)
                for j in range(4, 8):
                    l2_scale(j)

                def gate_silu(u, nth, dst):
                    dve.wait_ge(zt_ready, l * 8 + nth + 1)
                    dve.scalar_tensor_tensor(out=dst, in0=TM[2 + u % 2][:, :], scalar=1.0, in1=bank[u % 4][:, :],
                                             op0=ADD, op1=MUL).then_inc(bank_free[u % 4], 1)

                def fill(n):
                    u = U_CX + n
                    if n < 4:
                        shift_taps(l, u, XC[n][:, :], 4, lambda j: col(MP, M_LW + n * 4 + j), xc_ready, l * 4 + n + 1,
                                   lru_acc, l * 8 + 2 * n)
                    else:
                        gate_silu(u, n - 4, ZS[:, n - 4, :])

                def prep_1(c):
                    i = l * NC + c
                    dve.wait_ge(grow_done, i + 1)
                    dve.wait_ge(eg_ready, i + 1)
                    for h in range(NH):
                        s = slice(h * P, (h + 1) * P)
                        ins = dve.tensor_scalar(EL[:, c % 2, s], pb(c, 1)[:, s], col(GCS, c * 4 + h), 0.0, SUB, MAX)
                    ins.then_inc(el_pre, 1)

                def prep_2(c):
                    i = l * NC + c
                    dve.wait_ge(el_ready, i + 1)
                    dve.wait_ge(kk_done, i + 1)
                    if c >= 2:
                        dve.wait_ge(ta_done, i - 1)
                    for h in range(NH):
                        s = slice(h * P, (h + 1) * P)
                        ins = dve.scalar_tensor_tensor(out=DD[:, c, s], in0=pb(c, 2)[:, s],
                                                       scalar=col(BE, c * 4 + h), in1=EL[:, c % 2, s], op0=MUL, op1=MUL)
                    ins.then_inc(l_ready, 1)
                    dve.wait_ge(qk_done, i + 1)
                    dve.tensor_tensor(TM[2 + c % 2][:, :], pb(c, 3), EL[:, c % 2, :], MUL).then_inc(at_ready, 1)

                def start_blocks(c):
                    i = l * NC + c
                    dve.wait_ge(tl_done, i + 1)
                    dve.wait_ge(l_ready, i + 1)
                    dve.tensor_tensor(heads(DD[:, c, :]), heads(DD[:, c, :]), over_heads(neg_mask(0)), MUL)\
                       .then_inc(d_pre, 1)
                    dve.wait_ge(d_pre, i + 1)
                    dve.tensor_tensor(heads(DD[:, c, :]), heads(DD[:, c, :]), over_heads(ident), ADD)\
                       .then_inc(d_init, 1)

                def prep_3(c):
                    i = l * NC + c
                    dve.wait_ge(ta_done, i + 1)
                    dve.tensor_tensor(heads(ATT[:, c, :]), heads(pb(c, 2)), over_heads(upper), MUL)\
                       .then_inc(att_ready, 1)

                prep_1(0)
                fill(0)
                prep_1(1)
                prep_2(0)
                cum_weights(2)
                prep_2(1)
                prep_3(0)
                cum_weights(3)
                start_blocks(0)
                prep_1(2)
                start_blocks(1)
                prep_3(1)
                prep_2(2)
                prep_1(3)
                start_blocks(2)
                prep_3(2)
                prep_2(3)
                prep_3(3)
                start_blocks(3)

                def level_mask(n):
                    i = l * 24 + n
                    dve.wait_ge(y_done, i + 1)
                    if n >= 2:
                        dve.wait_ge(p_done, i - 1)
                    if n == 0:
                        dve.wait_ge(qd_ready, l * 4 + 4)
                    dve.tensor_tensor(heads(YM[:, n % 2, :]), heads(bank[4 + n % 2][:, :]),
                                      over_heads(neg_mask(1 + n // 4)), MUL).then_inc(ym_ready, 1)

                level_mask(0)
                for n in range(24):
                    if n + 1 < 24:
                        level_mask(n + 1)
                    c = n % 4
                    dve.wait_ge(p_done, l * 24 + n + 1)
                    if n < 20:
                        dve.tensor_tensor(DD[:, c, :], DD[:, c, :], bank[6][:, :], ADD).then_inc(d_upd, 1)
                    else:
                        dve.tensor_tensor(DTT[:, c, :], DTT[:, c, :], bank[7][:, :], ADD).then_inc(dt_fin, 1)

                for c in range(NC):
                    if c >= 1:
                        dve.wait_ge(ks_done, l * 3 + c)
                        dve.wait_ge(vn_done, l * 4 + c)
                        for h in range(NH):
                            s = slice(h * P, (h + 1) * P)
                            ins = dve.scalar_tensor_tensor(out=RR[:, s], in0=bank[4][:, s], scalar=col(NBG, c * 4 + h),
                                                           in1=VB[:, c, s], op0=MUL, op1=ADD)
                        ins.then_inc(r_ready, 1)
                    if c >= 1:
                        fill(2 * c)
                    if c < NC - 1:
                        new, old = ST[(c + 1) % 2], ST[c % 2]
                        dve.wait_ge(su_done, l * 3 + c + 1)
                        if c == 0:
                            dve.tensor_copy(new[:, :], bank[7][:, :]).then_inc(s_upd, 1)
                        else:
                            dve.wait_ge(s_upd, l * 3 + c)
                            for h in range(NH):
                                s = slice(h * P, (h + 1) * P)
                                ins = dve.scalar_tensor_tensor(out=new[:, s], in0=old[:, s], scalar=col(EGT, c * 4 + h),
                                                               in1=bank[7][:, s], op0=MUL, op1=ADD)
                            ins.then_inc(s_upd, 1)
                    fill(2 * c + 1)

                rows_inverse(l, 4, 1)
                for j in range(4):
                    dve.wait_ge(rn_b, l * 16 + 8 + j + 1)
                    dve.scalar_tensor_tensor(out=OT[:, j, :], in0=OT[:, j, :], scalar=col(MP, M_NW),
                                             in1=bank[6 + j % 2][:, :], op0=MUL, op1=MUL).then_inc(rn_app, 1)
                    dve.wait_ge(rn_app, l * 16 + 8 + j + 1)
                    dve.scalar_tensor_tensor(out=OT[:, j, :], in0=ZS[:, j, :], scalar=0.5, in1=OT[:, j, :],
                                             op0=MUL, op1=MUL).then_inc(y_fin, 1)

                def y_rest(nth, t, src):
                    dve.wait_ge(y_hi, l * 12 + nth + 1)
                    dve.tensor_tensor(Y[:, t, 1, :], src, Y[:, t, 0, :], SUB).then_inc(y_lo, 1)

                for i in range(4):
                    u = U_BQK + i
                    dve.wait_ge(raw_ready, l * 4 + i + 1)
                    dve.tensor_tensor(RQ[:, i, :], bank[u % 4][:, :], CS[:, 0, :], MUL).then_inc(bank_free[u % 4], 1)
                    v0 = l * 28 + i * 5
                    dve.wait_ge(lru_th, l * 4 + i + 1)
                    dve.tensor_scalar(INV[:, i, :], TH[:, i, :], 1.0, None, ADD).then_inc(lru_v, 1)
                    dve.wait_ge(lru_v, v0 + 1)
                    dve.reciprocal(INV[:, i, :], INV[:, i, :]).then_inc(lru_v, 1)
                    dve.scalar_tensor_tensor(out=TI[:, i, :], in0=TI[:, i, :], scalar=1.0, in1=XC[i][:, :],
                                             op0=ADD, op1=MUL).then_inc(lru_v, 1)
                    dve.wait_ge(lru_v, v0 + 3)
                    dve.tensor_tensor(TI[:, i, :], TI[:, i, :], INV[:, i, :], MUL).then_inc(lru_v, 1)
                    dve.wait_ge(lru_v, v0 + 4)
                    dve.tensor_scalar(INV[:, i, :], INV[:, i, :], 2.0, -1.0, MUL, ADD).then_inc(lru_v, 1)
                for i in range(4):
                    u = U_BQK + i
                    dve.wait_ge(perm_done, l * 4 + i + 1)
                    if i >= 2:
                        dve.wait_ge(rq_ready, l * 4 + i - 1)
                    dve.tensor_tensor(TM[i % 2][:, :], bank[4 + i % 2][:, :], CS[:, 1, :], MUL).then_inc(rot_m2, 1)
                    dve.wait_ge(rot_m2, l * 4 + i + 1)
                    dve.wait_ge(bank_free[u % 4], START + l * NBK + u // 4 + 1)
                    dve.tensor_tensor(RQ[:, i, :], RQ[:, i, :], TM[i % 2][:, :], ADD).then_inc(rq_ready, 1)
                for i in range(4):
                    y_rest(i, i, OT[:, i, :])

                def lru(j):
                    dve.wait_ge(lru_sq, l * 4 + j + 1)
                    dve.wait_ge(lru_v, l * 28 + 20 + 2 * j)
                    dve.tensor_tensor(TI[:, j, :], TI[:, j, :], TH[:, j, :], MUL).then_inc(lru_v, 1)
                    dve.wait_ge(lru_v, l * 28 + 20 + 2 * j + 1)
                    dve.tensor_tensor_scan(XC[j][:, :], INV[:, j, :], TI[:, j, :], 0.0, MUL, ADD).then_inc(lru_v, 1)

                def gelu_1(j):
                    t, b = TM[j % 2][:, :], bank[(U_CG + j) % 4][:, :]
                    dve.wait_ge(ge_a, l * 4 + j + 1)
                    dve.tensor_scalar(t, t, 0.044715, 1.0, MUL, ADD).then_inc(ge_v, 1)
                    dve.wait_ge(ge_v, l * 8 + 2 * j + 1)
                    dve.tensor_tensor(t, t, b, MUL).then_inc(ge_v, 1)

                def gelu_2(j):
                    u = U_CG + j
                    t, yt = TM[j % 2][:, :], TM[4 + j % 2][:, :]
                    dve.wait_ge(ge_t, l * 4 + j + 1)
                    dve.scalar_tensor_tensor(out=t, in0=t, scalar=1.0, in1=bank[u % 4][:, :],
                                             op0=ADD, op1=MUL).then_inc(bank_free[u % 4], 1)
                    dve.wait_ge(bank_free[u % 4], START + l * NBK + u // 4 + 1)
                    dve.wait_ge(lru_v, l * 28 + 20 + 2 * j + 2)
                    if j >= 2:
                        dve.wait_ge(y_lo, l * 12 + 4 + j - 1)
                    dve.scalar_tensor_tensor(out=yt, in0=t, scalar=0.5, in1=XC[j][:, :],
                                             op0=MUL, op1=MUL).then_inc(y_fin, 1)

                lru(0)
                gelu_1(0)
                for j in range(1, 4):
                    lru(j)
                    gelu_2(j - 1)
                    gelu_1(j)
                    y_rest(4 + j - 1, 8 + j - 1, TM[4 + (j - 1) % 2][:, :])
                gelu_2(3)
                y_rest(7, 11, TM[5][:, :])

                def scores(h, j):
                    n = h * 4 + j
                    off = sum(T - i * P for i in range(j))
                    dve.wait_ge(sc_done, l * 16 + n + 1)
                    if h >= 2 and j == 0:
                        dve.wait_ge(pv_done, l * 4 + h - 1)
                    dve.tensor_tensor(SC[h % 2][:, off:off + T - j * P], score_bank(n)[:, 0:T - j * P],
                                      CO[:, C_DM + h * T:C_DM + (h + 1) * T - j * P], MUL).then_inc(sc_ready, 1)

                def bg(h):
                    u = U_BG + h
                    gate_silu(u, 4 + h, BGS[:, h, :])

                bg(0)
                for j in range(4):
                    scores(0, j)
                bg(1)
                for j in range(3):
                    scores(1, j)
                bg(2)
                scores(1, 3)
                for j in range(2):
                    scores(2, j)
                bg(3)
                for j in range(2, 4):
                    scores(2, j)
                for j in range(4):
                    scores(3, j)
                for h in range(NH):
                    dve.wait_ge(mean_done, l * 4 + h + 1)
                    dve.scalar_tensor_tensor(out=OB[:, h, :], in0=bank[5 + h % 2][:, :], scalar=-1.0 / P,
                                             in1=OB[:, h, :], op0=MUL, op1=ADD).then_inc(cen_ready, 1)
                rows_inverse(l, 4, 2)
                dve.wait_ge(bank_free[(U_BG + 3) % 4], START + l * NBK + (U_BG + 3) // 4 + 1)
                for j in range(4):
                    dve.wait_ge(rn_b, l * 16 + 12 + j + 1)
                    dve.tensor_tensor(OB[:, j, :], OB[:, j, :], bank[6 + j % 2][:, :], MUL).then_inc(rn_app, 1)
                    dve.wait_ge(rn_app, l * 16 + 12 + j + 1)
                    dve.scalar_tensor_tensor(out=OB[:, j, :], in0=BGS[:, j, :], scalar=0.5, in1=OB[:, j, :],
                                             op0=MUL, op1=MUL).then_inc(y_fin, 1)
                    if j >= 2:
                        y_rest(8 + j - 2, 4 + j - 2, OB[:, j - 2, :])
                for h in range(2, 4):
                    y_rest(8 + h, 4 + h, OB[:, h, :])

                for d in range(DT_):
                    if d == DT_ - 1:
                        for k in range(0, 6, 2):
                            h_rest(l, 1, k, MM)
                    dve.wait_ge(gemm_done, START + l * NU + U_MIX + 4 * d + 4)
                    for n in range(3):
                        dve.wait_ge(bank_free[n], START + l * NBK + (U_MIX + 4 * d) // 4 + 1)
                    dve.scalar_tensor_tensor(out=MM[:, d, :], in0=GT[:, d % 2, 0, :], scalar=1.0, in1=bank[3][:, :],
                                             op0=ADD, op1=MUL).then_inc(bank_free[3], 1)
                    dve.scalar_tensor_tensor(out=TM[0][:, :], in0=GT[:, d % 2, 1, :], scalar=1.0, in1=bank[4][:, :],
                                             op0=ADD, op1=MUL).then_inc(mg_v, 1)
                    if d >= 1:
                        dve.wait_ge(hn_ready, l * 24 + 8 + d)
                    dve.scalar_tensor_tensor(out=TM[1][:, :], in0=GT[:, d % 2, 2, :], scalar=1.0, in1=bank[5][:, :],
                                             op0=ADD, op1=MUL).then_inc(mg_done, 1)
                    dve.wait_ge(mg_v, l * 16 + 2 * d + 1)
                    dve.wait_ge(bank_free[3], START + l * NBK + (U_MIX + 4 * d) // 4 + 1)
                    dve.tensor_tensor(MM[:, d, :], MM[:, d, :], TM[0][:, :], ADD).then_inc(mg_v, 1)
                    dve.wait_ge(mg_v, l * 16 + 2 * d + 2)
                    dve.wait_ge(mg_done, l * 8 + d + 1)
                    dve.tensor_tensor(MM[:, d, :], MM[:, d, :], TM[1][:, :], ADD).then_inc(hn_ready, 1)
                h_rest(l, 1, 6, MM)
                for d in range(DT_):
                    u = U_OUT + d
                    dve.wait_ge(gemm_done, START + l * NU + u + 1)
                    dve.scalar_tensor_tensor(out=X[:, d, :], in0=bank[u % 4][:, :], scalar=0.5, in1=X[:, d, :],
                                             op0=MUL, op1=ADD).then_inc(bank_free[u % 4], 1)
                    if d >= 2:
                        square_sum(l, 1, d - 1)
                for b in range(4):
                    dve.wait_ge(bank_free[b], START + l * NBK + (U_OUT + 7) // 4 + 1)
                norm_apply(l, 1, M_GF, 2)

                dve.wait_ge(ld_fp, l * 16 + 16)
                p0 = 0
                for g in range(2):
                    for i in range(PAIRS[g]):
                        p, u = p0 + i, U_FFN[g] + 2 * i
                        shift_taps(l, u, CG[:, p % 2, :], 3, lambda j: col(FP, F_W + p * 3 + j), fc_ready,
                                   l * 44 + 2 * p + 1, fc_acc, l * 44 + 2 * p)
                        dve.wait_ge(ft_ready, l * 22 + p + 1)
                        dve.scalar_tensor_tensor(out=CG[:, p % 2, :], in0=TG[:, p % 2, :], scalar=1.0,
                                                 in1=CG[:, p % 2, :], op0=ADD, op1=MUL).then_inc(fg_v, 1)
                        shift_taps(l, u + 1, CV[:, p % 2, :], 3, lambda j: col(FP, F_W + (22 + p) * 3 + j), fc_ready,
                                   l * 44 + 2 * p + 2, fc_acc, l * 44 + 2 * p + 1)
                        dve.wait_ge(fg_v, l * 22 + p + 1)
                        dve.wait_ge(bank_free[(u + 1) % 4], START + l * NBK + (u + 1) // 4 + 1)
                        dve.scalar_tensor_tensor(out=CV[:, p % 2, :], in0=CG[:, p % 2, :], scalar=0.5,
                                                 in1=CV[:, p % 2, :], op0=MUL, op1=MUL).then_inc(fg_done, 1)
                        dve.wait_ge(f_hi, l * 22 + p + 1)
                        dve.tensor_tensor(Y[:, i, 1, :], CV[:, p % 2, :], Y[:, i, 0, :], SUB).then_inc(f_lo, 1)
                    for d in range(DT_):
                        u = U_DOWN[g] + d
                        dve.wait_ge(gemm_done, START + l * NU + u + 1)
                        dve.tensor_tensor(X[:, d, :], X[:, d, :], bank[u % 4][:, :], ADD).then_inc(bank_free[u % 4], 1)
                        if g == 1 and d >= 2:
                            square_sum(l + 1, 0, d - 1)
                    p0 += PAIRS[g]
                for b in range(4):
                    dve.wait_ge(bank_free[b], START + l * NBK + NBK)

            dve.wait_ge(ld_const, 32)
            norm_inverse(L, 0)
            for k in range(KT):
                dve.scalar_tensor_tensor(out=HN[:, k, :], in0=X[:, k, :], scalar=col(FN, k), in1=bank[6][:, :],
                                         op0=MUL, op1=MUL).then_inc(out_ready, 1)


def shape_constants():
    import numpy as np
    i = np.arange(P)
    c = np.zeros((P, NCONST), np.float32)
    c[:, C_ID:C_ID + P] = np.eye(P)
    c[:, C_ONE:C_ONE + P] = 1
    c[:, C_U:C_U + P] = i[:, None] <= i[None, :]
    for h in range(2):
        for m in range(32):
            c[64 * h + m + 32, C_PERM + 64 * h + m] = -1
            c[64 * h + m, C_PERM + 64 * h + m + 32] = 1
    for lv in range(7):
        s = 1 << lv
        m = (i[:, None] // (2 * s) == i[None, :] // (2 * s)) & (i[:, None] // s > i[None, :] // s)
        c[:, C_NEG + lv * P:C_NEG + (lv + 1) * P] = -m.astype(np.float32)
        if lv == 0:
            c[:, C_M1T:C_M1T + P] = -m.T.astype(np.float32)
    lg = np.log(np.float32(1.0) - np.float32(2.0) ** (-5.0 - np.arange(NH, dtype=np.float32))).astype(np.float64)
    x = np.arange(T)
    for h in range(NH):
        d = x[None, :] - i[:, None]
        c[:, C_DM + h * T:C_DM + (h + 1) * T] = np.where(d >= 0, np.exp(np.maximum(d, 0) * lg[h]) * 64 ** -0.5, 0)
    c[:, C_MISC] = (np.float32(10000.0) ** (-(i % 32).astype(np.float32) / np.float32(32))).astype(np.float32)
    c[:, C_MISC + 1:C_MISC + 4] = P * 4 * EPS, 4 * EPS, EPS
    return c


def kernel(**inp):
    import numpy as np
    from concourse import bacc
    from concourse.bass_utils import run_bass_kernel_spmd as run

    a = {k: np.asarray(v) for k, v in inp.items()}

    def cols(v, n):
        return v.reshape(n, P).T

    def w_units(w):
        k, n = w.shape[0] // P, w.shape[1] // P
        return w.reshape(k, P, n, P).transpose(2, 1, 0, 3).reshape(n, P, k * P)

    wst = np.zeros((L * NU, P, SLOT), np.float32)
    mp = np.zeros((L, P, NMP), np.float32)
    fp = np.zeros((L, P, NFP), np.float32)
    for l in range(L):
        def put(u, units):
            wst[l * NU + u:l * NU + u + len(units), :, :units.shape[2]] = units
        w = a["w_in"][l]
        o = {"qkv": 0, "ab": 1536, "z": 1544, "bq": 2056, "bk": 2312, "bv": 2568, "bg": 3080, "cx": 3592, "cg": 4104,
             "gate": 4616}
        put(U_QKV, w_units(w[:, 0:1536]))
        put(U_Z, w_units(w[:, o["z"]:o["z"] + 512]))
        put(U_BG, w_units(w[:, o["bg"]:o["bg"] + 512]))
        put(U_BQK, w_units(w[:, o["bq"]:o["bq"] + 512]))
        put(U_BV, w_units(w[:, o["bv"]:o["bv"] + 512]))
        put(U_CX, w_units(w[:, o["cx"]:o["cx"] + 512]))
        put(U_CG, w_units(w[:, o["cg"]:o["cg"] + 512]))
        gates = w_units(w[:, o["gate"]:])
        br = w_units(a["w_branch"][l].reshape(12 * P, D))
        for d in range(DT_):
            for n in range(3):
                put(U_MIX + 4 * d + n, gates[8 * n + d][None])
            put(U_MIX + 4 * d + 3, br[d][None])
        put(U_OUT, w_units(a["w_out"][l]))
        up, down = w_units(a["w_up"][l]), a["w_down"][l]
        p0 = 0
        for g in range(2):
            for i in range(PAIRS[g]):
                put(U_FFN[g] + 2 * i, up[p0 + i][None])
                put(U_FFN[g] + 2 * i + 1, up[22 + p0 + i][None])
            put(U_DOWN[g], w_units(down[p0 * P:(p0 + PAIRS[g]) * P]))
            p0 += PAIRS[g]
        m = mp[l]
        m[:, M_GA:M_GA + 8] = cols(a["attn_norm"][l], 8)
        m[:, M_GF:M_GF + 8] = cols(a["ffn_norm"][l], 8)
        m[:, M_CW:M_CW + 48] = a["dn_conv_w"][l].reshape(4, 12, P).transpose(2, 1, 0).reshape(P, 48)
        m[:, M_NW] = a["dn_norm_w"][l]
        m[:, M_LW:M_LW + 16] = a["lru_conv_w"][l].reshape(4, 4, P).transpose(2, 1, 0).reshape(P, 16)
        m[:, M_LB:M_LB + 4] = cols(a["lru_conv_b"][l], 4)
        m[:, M_BA:M_BA + 4] = a["lru_ba"][l].T
        m[:, M_BX:M_BX + 4] = a["lru_bx"][l].T
        m[:, M_LAM:M_LAM + 4] = cols(a["lru_lambda"][l], 4)
        m[:, M_DT:M_DT + 4] = a["dn_dt_bias"][l][None]
        m[:, M_ALOG:M_ALOG + 4] = a["dn_a_log"][l][None]
        m[:, M_WAB:M_WAB + 64] = w[:, 1536:1544].reshape(8, P, 8).transpose(1, 0, 2).reshape(P, 64)
        m[:, M_WA:M_WA + 512] = a["lru_wa"][l].transpose(1, 0, 2).reshape(P, 512)
        m[:, M_WX:M_WX + 512] = a["lru_wx"][l].transpose(1, 0, 2).reshape(P, 512)
        fp[l, :, F_W:F_W + 132] = a["ffn_conv_w"][l].reshape(3, 44, P).transpose(2, 1, 0).reshape(P, 132)
        fp[l, :, F_B:F_B + 44] = cols(a["ffn_conv_b"][l], 44)
    arrays = {
        "consts": shape_constants(),
        "pos": np.ascontiguousarray(np.broadcast_to(a["positions"], (P, T))),
        "x": np.ascontiguousarray(a["x"][0].T.reshape(KT, P, T).transpose(1, 0, 2)),
        "wst": wst, "mp": mp, "fp": fp, "fn": np.ascontiguousarray(cols(a["final_norm"], 8)),
    }
    nc = bacc.Bacc("TRN2", target_bir_lowering=False, num_devices=1, dynamic_dma_scratch_size=1024)
    aps = [nc.dram_tensor(n, list(v.shape), mybir.dt.from_np(v.dtype), kind="ExternalInput").ap()
           for n, v in arrays.items()]
    o = nc.dram_tensor("out", [P, KT, T], F32, kind="ExternalOutput").ap()
    nc.disable_value_cache = True
    build(nc, *aps, o)
    r = np.asarray(run(nc, [arrays], core_ids=[0]).results[0]["out"])
    return np.ascontiguousarray(r.transpose(1, 0, 2).reshape(D, T).T)[None]
```
